# Optimizing a Trainium2 kernel written in Bass

```python
import math
import jax
import jax.numpy as jnp
from jax import lax
import numpy as np

D_MODEL = 1024
BATCH = 1
SEQ = 256
DEPTH = 1

MIX_WIDTH = D_MODEL
HGRN_WIDTH = MIX_WIDTH // 2
HGRN_HEADS = 4
HGRN_HEAD_V = HGRN_WIDTH // HGRN_HEADS
HGRN_HEAD_K = 128
HGRN_KEY = HGRN_HEADS * HGRN_HEAD_K
CONV_CH = MIX_WIDTH - HGRN_WIDTH
CONV_LEN = 31
CHUNK = 64
SUB_CHUNK = 16
N_EXPERTS = 32
TOP_K = 4
D_FF = D_MODEL
SWIGLU_LIMIT = 7.0
SWIGLU_ALPHA = 1.702
MOE_BLOCK = 256
EPS = 1e-5
IN_COLS = 3 * HGRN_KEY + 2 * HGRN_WIDTH + 2 * CONV_CH

kernel_name = "hybrid_hgrn2_conformer_moe_encoder"

def _rmsnorm(x, w):
    xf = x.astype(jnp.float32)
    y = xf * lax.rsqrt(jnp.mean(xf * xf, axis=-1, keepdims=True) + EPS)
    return (y * w).astype(x.dtype)

def _chunk_recurrence(q, k, v, logf):
    bn, nh, t_len, dk = q.shape
    dv = v.shape[-1]
    n_ch = t_len // CHUNK
    ns = CHUNK // SUB_CHUNK
    q, k, logf = [a.reshape(bn, nh, n_ch, CHUNK, dk) for a in (q, k, logf)]
    v = v.reshape(bn, nh, n_ch, CHUNK, dv)
    b = jnp.cumsum(logf, axis=3)
    b_end = b[:, :, :, -1:, :]
    k_to_end = k * jnp.exp(b_end - b)
    u = jnp.einsum('bhncd,bhnce->bhnde', k_to_end, v)
    decay = jnp.exp(b_end[:, :, :, 0, :])

    def step(state, inp):
        dec_n, u_n = inp
        return dec_n[..., None] * state + u_n, state

    s0 = jnp.zeros((bn, nh, dk, dv), jnp.float32)
    _, s_prev = lax.scan(step, s0, (jnp.moveaxis(decay, 2, 0), jnp.moveaxis(u, 2, 0)))
    o_inter = jnp.einsum('bhncd,nbhde->bhnce', q * jnp.exp(b), s_prev)
    bs = b.reshape(bn, nh, n_ch, ns, SUB_CHUNK, dk)
    qs = q.reshape(bn, nh, n_ch, ns, SUB_CHUNK, dk)
    ks = k.reshape(bn, nh, n_ch, ns, SUB_CHUNK, dk)
    e_sub = bs[:, :, :, :, -1, :]
    k_sub = ks * jnp.exp(e_sub[:, :, :, :, None, :] - bs)
    q_rel = q[:, :, :, :, None, :] * jnp.exp(
        jnp.minimum(b[:, :, :, :, None, :] - e_sub[:, :, :, None, :, :], 0.0))
    a_off = jnp.einsum('bhntjd,bhnjsd->bhntjs', q_rel, k_sub).reshape(bn, nh, n_ch, CHUNK, CHUNK)
    tri = jnp.tril(jnp.ones((SUB_CHUNK, SUB_CHUNK), bool))
    diff = bs[..., :, None, :] - bs[..., None, :, :]
    dec = jnp.exp(jnp.where(tri[:, :, None], diff, -jnp.inf))
    a_diag = jnp.einsum('bhnitd,bhnisd,bhnitsd->bhnits', qs, ks, dec)
    a_diag_full = jnp.einsum('bhnits,ij->bhnitjs', a_diag,
                             jnp.eye(ns, dtype=a_diag.dtype)).reshape(bn, nh, n_ch, CHUNK, CHUNK)
    sub_id = jnp.arange(CHUNK) // SUB_CHUNK
    off_mask = sub_id[:, None] > sub_id[None, :]
    a = jnp.where(off_mask, a_off, 0.0) + a_diag_full
    o_intra = jnp.einsum('bhnts,bhnse->bhnte', a, v)
    return (o_inter + o_intra).reshape(bn, nh, t_len, dv)

def _hgrn2_mixer(qz, fz_f, fz_b, iv, gz, lb_f, lb_b, norm_w):
    bn, t_len, _ = qz.shape

    def heads(a, d):
        return a.reshape(bn, t_len, HGRN_HEADS, d).transpose(0, 2, 1, 3).astype(jnp.float32)

    q = jax.nn.silu(heads(qz, HGRN_HEAD_K))
    v = heads(iv, HGRN_HEAD_V)

    def gate(fz, lb):
        lb = lb.astype(jnp.float32).reshape(HGRN_HEADS, 1, HGRN_HEAD_K)
        f = lb + (1.0 - lb) * jax.nn.sigmoid(heads(fz, HGRN_HEAD_K))
        return jnp.log(f), 1.0 - f

    logf_f, k_f = gate(fz_f, lb_f)
    logf_b, k_b = gate(fz_b, lb_b)
    o_f = _chunk_recurrence(q, k_f, v, logf_f)
    flip = lambda a: jnp.flip(a, axis=2)
    o_b = flip(_chunk_recurrence(flip(q), flip(k_b), flip(v), flip(logf_b)))
    o = o_f + o_b
    o = o * lax.rsqrt(jnp.mean(o * o, axis=-1, keepdims=True) + EPS)
    o = o.transpose(0, 2, 1, 3).reshape(bn, t_len, HGRN_WIDTH) * norm_w
    return (o * jax.nn.silu(gz.astype(jnp.float32))).astype(qz.dtype)

def _conformer_conv(cv, cg, dw_w, dw_b, ln_w, ln_b):
    u = cv * jax.nn.sigmoid(cg)
    pad = (CONV_LEN - 1) // 2
    u = lax.conv_general_dilated(
        u, dw_w.reshape(CONV_LEN, 1, CONV_CH).astype(u.dtype), window_strides=(1,),
        padding=[(pad, pad)], dimension_numbers=('NWC', 'WIO', 'NWC'),
        feature_group_count=CONV_CH) + dw_b
    uf = u.astype(jnp.float32)
    mu = jnp.mean(uf, axis=-1, keepdims=True)
    var = jnp.mean(jnp.square(uf - mu), axis=-1, keepdims=True)
    uf = (uf - mu) * lax.rsqrt(var + EPS) * ln_w + ln_b
    return jax.nn.silu(uf).astype(cv.dtype)

def _moe(xf, router_w, router_b, w1, b1, w2, b2):
    t_tok, d = xf.shape
    tk = t_tok * TOP_K
    logits = (xf @ router_w + router_b).astype(jnp.float32)
    top_val, top_idx = lax.top_k(logits, TOP_K)
    gates = jax.nn.softmax(top_val, axis=-1)
    flat_e = top_idx.reshape(-1).astype(jnp.int32)
    flat_tok = jnp.repeat(jnp.arange(t_tok, dtype=jnp.int32), TOP_K)
    order = jnp.argsort(flat_e)
    sorted_e = flat_e[order]
    counts = jnp.bincount(flat_e, length=N_EXPERTS)
    padded = ((counts + MOE_BLOCK - 1) // MOE_BLOCK) * MOE_BLOCK
    pad_end = jnp.cumsum(padded)
    pad_start = pad_end - padded
    grp_start = jnp.cumsum(counts) - counts
    rank = jnp.arange(tk, dtype=jnp.int32) - grp_start[sorted_e]
    dest = pad_start[sorted_e] + rank
    n_blocks = -(-tk // MOE_BLOCK) + N_EXPERTS
    rows = n_blocks * MOE_BLOCK
    src_tok = jnp.zeros((rows,), jnp.int32).at[dest].set(flat_tok[order])
    row_gate = jnp.zeros((rows,), jnp.float32).at[dest].set(gates.reshape(-1)[order])
    block_start = jnp.arange(n_blocks, dtype=pad_end.dtype) * MOE_BLOCK
    block_expert = jnp.minimum(jnp.searchsorted(pad_end, block_start, side='right'),
                               N_EXPERTS - 1).astype(jnp.int32)
    xs = xf[src_tok].reshape(n_blocks, MOE_BLOCK, d)

    def expert_block(args):
        xb, e = args
        hdn = xb @ w1[e] + b1[e]
        h_glu = jnp.minimum(hdn[:, :D_FF], SWIGLU_LIMIT)
        h_lin = jnp.clip(hdn[:, D_FF:], -SWIGLU_LIMIT, SWIGLU_LIMIT)
        act = h_glu * jax.nn.sigmoid(SWIGLU_ALPHA * h_glu) * (h_lin + 1.0)
        return act @ w2[e] + b2[e]

    ys = lax.map(expert_block, (xs, block_expert)).reshape(rows, d)
    ys = (ys.astype(jnp.float32) * row_gate[:, None]).astype(xf.dtype)
    return jnp.zeros((t_tok, d), xf.dtype).at[src_tok].add(ys)

def setup_inputs(seed: int = 0) -> dict:
    key = jax.random.key(seed)
    ks = jax.random.split(key, 20)
    nrm = lambda k, s: jax.random.normal(k, s, jnp.float32)
    return {
        "x": nrm(ks[0], (BATCH, SEQ, D_MODEL)),
        "norm1_w": 1.0 + 0.02 * nrm(ks[1], (DEPTH, D_MODEL)),
        "w_in": nrm(ks[2], (DEPTH, D_MODEL, IN_COLS)) * D_MODEL ** -0.5,
        "lb_logits": 0.1 * nrm(ks[3], (2, DEPTH + 1, HGRN_KEY)),
        "hgrn_norm_w": 1.0 + 0.02 * nrm(ks[4], (DEPTH, HGRN_WIDTH)),
        "dw_w": nrm(ks[5], (DEPTH, CONV_LEN, CONV_CH)) * CONV_LEN ** -0.5,
        "dw_b": 0.01 * nrm(ks[6], (DEPTH, CONV_CH)),
        "conv_ln_w": 1.0 + 0.02 * nrm(ks[7], (DEPTH, CONV_CH)),
        "conv_ln_b": 0.01 * nrm(ks[8], (DEPTH, CONV_CH)),
        "w_out": nrm(ks[9], (DEPTH, MIX_WIDTH, D_MODEL)) * MIX_WIDTH ** -0.5,
        "norm2_w": 1.0 + 0.02 * nrm(ks[10], (DEPTH, D_MODEL)),
        "router_w": nrm(ks[11], (DEPTH, D_MODEL, N_EXPERTS)) * D_MODEL ** -0.5,
        "router_b": 0.01 * nrm(ks[12], (DEPTH, N_EXPERTS)),
        "w1": nrm(ks[13], (DEPTH, N_EXPERTS, D_MODEL, 2 * D_FF)) * D_MODEL ** -0.5,
        "b1": 0.01 * nrm(ks[14], (DEPTH, N_EXPERTS, 2 * D_FF)),
        "w2": nrm(ks[15], (DEPTH, N_EXPERTS, D_FF, D_MODEL)) * D_FF ** -0.5,
        "b2": 0.01 * nrm(ks[16], (DEPTH, N_EXPERTS, D_MODEL)),
        "final_norm_w": 1.0 + 0.02 * nrm(ks[17], (D_MODEL,)),
    }

def reference(x, norm1_w, w_in, lb_logits, hgrn_norm_w, dw_w, dw_b, conv_ln_w, conv_ln_b,
              w_out, norm2_w, router_w, router_b, w1, b1, w2, b2, final_norm_w):
    bn, t_len, d = x.shape
    lb_table = jnp.cumsum(jax.nn.softmax(lb_logits.astype(jnp.float32), axis=1), axis=1)
    splits = list(np.cumsum([HGRN_KEY, HGRN_KEY, HGRN_KEY, HGRN_WIDTH, HGRN_WIDTH, CONV_CH]))
    h = x
    for l in range(DEPTH):
        n = _rmsnorm(h, norm1_w[l])
        proj = n @ w_in[l]
        qz, fz_f, fz_b, iv, gz, cv, cg = jnp.split(proj, splits, axis=-1)
        a_out = _hgrn2_mixer(qz, fz_f, fz_b, iv, gz, lb_table[0, l], lb_table[1, l], hgrn_norm_w[l])
        b_out = _conformer_conv(cv, cg, dw_w[l], dw_b[l], conv_ln_w[l], conv_ln_b[l])
        h = h + jnp.concatenate([a_out, b_out], axis=-1) @ w_out[l]
        n2 = _rmsnorm(h, norm2_w[l])
        h = h + _moe(n2.reshape(bn * t_len, d), router_w[l], router_b[l],
                     w1[l], b1[l], w2[l], b2[l]).reshape(bn, t_len, d)
    return _rmsnorm(h, final_norm_w)


_drawn_inputs = setup_inputs


def setup_inputs(seed=0):
    import zlib

    import numpy as np

    out = dict(_drawn_inputs(seed))
    spreads = {}
    factors = {'lb_logits': 3.089,
     'conv_ln_b': 3.578,
     'b1': 8.0,
     'b2': 8.0,
     'final_norm_w': 8.253,
     'dw_b': 2.91}
    for name, (base, spread) in spreads.items():
        noise = np.random.default_rng([zlib.crc32(name.encode()), seed]).standard_normal(out[name].shape)
        drawn = base * np.exp(spread * noise) if base else spread * noise
        out[name] = jnp.asarray(drawn.astype(out[name].dtype))
    for name, factor in factors.items():
        out[name] = (out[name] * factor).astype(out[name].dtype)
    return out
```

```python
import concourse.bass as bass
from concourse import mybir
from contextlib import ExitStack

F32 = mybir.dt.float32
F32R = mybir.dt.float32r
I32 = mybir.dt.int32
U8 = mybir.dt.uint8
ALU = mybir.AluOpType
ACT = mybir.ActivationFunctionType
AX = mybir.AxisListType

P = 128
T = 256
NT = T // P
D = 1024
C = D // P
H = 4
CH = 4
TAPS = 31
PAD = TAPS // 2
E = 32
TOPK = 4
CW = 512
SLOTS = 6
BLK = 64
EXTRA = (T * TOPK + E * (BLK - 1)) // BLK - E
LIMIT = 7.0
ALPHA = 1.702
EPS = 1e-5
HUGE = 3.0e38

CV, CG, FF, QZ, FB, IV, GZ = range(7)
W_IN_COLUMNS = [5, 6, 1, 0, 2, 3, 4]
N_IN = 7
N_FRONT = N_IN + 2
N_EXP = 6
LEVELS = [64, 32, 16, 8, 4, 2, 1]
UNITS = 2 * N_EXP
ORDER = [(j, a) for j in range(4) for a in (0, 1)] + [(4, 0), (5, 0), (4, 1), (5, 1)]
DONE = [max(i for i, u in enumerate(ORDER) if u[0] == j) + 1 for j in range(N_EXP)]
NPC = 4
PRM = 40
WD = 3

K_ID, K_ID2, K_IOTA, K_TRI = 0, 128, 192, 448
K_END = 576


def encoder_layer(nc, x, w_in, w_out, w1, w2, prm, dww, b1, b2, router_w, router_b,
                  norm2_w, final_w, consts, masks, out):
    w_in_v = w_in.rearrange("(c p) n -> p c n", p=P)
    w_out_v = w_out.rearrange("(c p) n -> p c n", p=P)
    w1_v = w1.rearrange("e (c p) n -> e p c n", p=P)
    w2_v = w2.rearrange("e (c p) n -> e p c n", p=P)
    x_v = x.rearrange("(i p) d -> p i d", p=P)
    out_v = out.rearrange("(i p) d -> p i d", p=P)

    keep = ExitStack()
    front = ExitStack()

    def sb(name, shape, dt=F32, stack=keep):
        return stack.enter_context(nc.sbuf_tensor(name, shape, dt))

    def sem(name):
        return keep.enter_context(nc.semaphore(name))

    with keep:
        ring = sb("ring", [P, SLOTS, C, CW])
        h = sb("h", [P, NT, D])
        n2 = sb("n2", [P, NT, D])
        cst = sb("cst", [P, K_END])
        wrow = sb("wrow", [P, D])
        b1T = sb("b1T", [P, 2 * C, E])
        gates = sb("gates", [P, NT, E])
        rankm = sb("rankm", [P, NT, E])
        table = sb("table", [1, 2, 16], I32)
        nextra = sb("nextra", [1, 1], I32)
        eps = sb("eps", [P, 1])
        ones = sb("ones", [P, T])
        ones_v = sb("ones_v", [P, P])
        ones_c = sb("ones_c", [P, P])
        ssum = sb("ssum", [P, 8])
        ident = cst[:, K_ID:K_ID + P]
        ident2 = cst[:, K_ID2:K_ID2 + BLK]
        iota = cst[:, K_IOTA:K_IOTA + T]
        tri = cst[:, K_TRI:K_TRI + P]

        nT = sb("nT", [P, C, T], stack=front)
        msk = sb("msk", [P, 2 * len(LEVELS) + 1, P], U8, front)
        q = sb("q", [P, H, T], stack=front)
        kf = sb("kf", [P, H, T], stack=front)
        kb = sb("kb", [P, H, T], stack=front)
        bf = sb("bf", [P, H, T], stack=front)
        bb = sb("bb", [P, H, T + 1], stack=front)
        v = sb("v", [P, NT, CW], stack=front)
        gate = sb("gate", [P, H, T], stack=front)
        cv = sb("cv", [P, CH, T], stack=front)
        u = sb("u", [P, CH, T + 2 * PAD], stack=front)
        acc = sb("acc", [P, CH, T], stack=front)
        ex = sb("ex", [P, 2, H, T], stack=front)
        wk = sb("wk", [P, 2, H, T], stack=front)
        am = sb("am", [P, H, NT, P], stack=front)
        off = sb("off", [P, 2, H, P], stack=front)
        cat = sb("cat", [P, C, T], stack=front)
        dwT = sb("dwT", [P, TAPS * CH], stack=front)
        prmT = sb("prmT", [P, PRM], stack=front)
        n1w = prmT[:, 32:32 + C]
        rw = sb("rw", [P, C, E], stack=front)
        rb = sb("rb", [1, E], stack=front)
        lbs = sb("lbs", [P, 6, 2, H], stack=front)
        lg = sb("lg", [P, NT, E], stack=front)
        mx = sb("mx", [P, NT, 8], stack=front)
        sm = sb("sm", [P, 8, NT], stack=front)
        flat = "p h t -> p (h t)"
        rt = bf[:].rearrange(flat)[:, 0:8 * NT * E].rearrange("p (k i e) -> p k i e", k=8, i=NT)
        gT = kb[0:E, 0, :]
        ctf = q[0:1].rearrange(flat)[:, 0:4 * E].rearrange("p (k e) -> p k e", k=4)
        eb = q[0:1].rearrange(flat)[:, 512:576].rearrange("p (k j) -> p k j", k=4)
        cmp_ = kf[0:1].rearrange(flat)[:, 0:2 * EXTRA * E].rearrange("p (k j e) -> p k j e", k=2, j=EXTRA)
        msk_f = ex[:].rearrange("p a h t -> p (a h t)")[:, 0:(2 * len(LEVELS) + 1) * P]\
            .rearrange("p (m t) -> p m t", t=P)
        sA = cat[:, 0:4, :]
        sB = cat[:, 4:8, :]
        b1_rows = cat[0:E, :, :].rearrange("p a b -> p (a b)")
        b2_rows = cv[0:E, :, :].rearrange("p a b -> p (a b)")
        rows = u[:, 0, 0:256].rearrange("p (a b) -> p a b", b=P)
        front.close()

        wh = sb("wh", [P, WD, 4, CW], F32R)
        wl = sb("wl", [P, WD, 4, CW], F32R)
        xg = sb("xg", [P, C, 2 * BLK], F32R)
        aT = sb("aT", [P, C, 2 * BLK], F32R)
        hid = sb("hid", [P, 2, CW])
        y = sb("y", [P, D])
        pre = sb("pre", [P, 2, 4, BLK])
        glu = sb("glu", [P, 4, BLK])
        lin = sb("lin", [P, 4, BLK])
        sig = sb("sig", [P, 4, BLK])
        gs = sb("gs", [P, 4, BLK])
        act_ = sb("act_", [P, 4, BLK])
        sel = sb("sel", [P, NT, BLK])
        selg = sb("selg", [P, NT, 2, BLK])
        gsel = sb("gsel", [P, NT, P])
        cur = sb("cur", [P, 4, NT])

        ps = keep.enter_context(nc.psum_tensor("ps", [P, 8, 512], F32))

        def pair(i):
            return ps[:, 2 * i:2 * i + 2, :].rearrange("p a b -> p (a b)")

        def heads(ap):
            return ap.rearrange("p (h t) -> p h t", h=4)

        full = [sem(f"ring_full{s}") for s in range(SLOTS)]
        x_in, c_in, m_in, p_in, b1_in, b2_in, w2r_in, fw_in, r_in = [sem(n) for n in (
            "x_in", "consts_in", "masks_in", "params_in", "b1_in", "b2_in",
            "norm2_in", "final_in", "router_in")]
        (fills, sq1, rms1, xn_ok, xT_ok, nT_act, nT_dve, prm_ps, prm_sb, proj, ev_act, ev_dve,
         f_ok, logf_ok, sc_ok, e_ok, exp_ok, w_ok, prod, lev, ksum_ok, ksum_in) = [sem(n) for n in (
             "fills", "squares1", "rms1", "xn_ready", "xT_in_psum", "nT_by_act", "nT_by_dve",
             "params_in_psum", "params_ready", "projected", "evacuated_by_act", "evacuated_by_dve",
             "gate_ready", "log_gate_ready", "prefix_ready", "exponents_ready", "exps_ready",
             "scaled_ready", "level_products", "levels_merged", "key_sum_ready", "keys_ready")]
        (conv_ok, mu_ps, xc_ok, xc2_ok, var_ps, std_ok, ln_ok, lsg_ok, catb_ok) = [sem(n) for n in (
            "conv_ready", "conv_mean", "conv_centred", "conv_squares", "conv_var",
            "conv_std", "conv_normed", "conv_sigmoid", "cat_conv_ready")]
        (av, o2_ok, oms_ps, ostd_ok, cata_ok, wout_done, oproj, h_ok, sq2, rms2, n2_ok, n2T_ps, n2T_sb,
         lgt_ps, lg_ok, ex4_ok, sel_ok, rank_ps, gates_ok, gT_ps, gT_sb, acc0, routed) = [sem(n) for n in (
             "attended", "o_squares", "o_mean_square", "o_rms", "cat_heads_ready", "w_out_used",
             "out_projected", "h_ready", "squares2", "rms2", "n2_ready", "n2T_in_psum", "n2T_ready",
             "logits_in_psum", "logits_ready", "gate_exps", "chosen_ready", "ranks_in_psum",
             "gates_ready", "gatesT_in_psum", "gatesT_ready", "b2_summed", "routed")]
        (s_sel, s_selg, s_xps, s_xh, s_xl, s_wh, s_wl, s_mm, s_ev, s_tr, s_pre, s_glu, s_sig, s_gs,
         s_act, s_ah, s_al, s_gps, s_gt, s_comb, s_cur, s_lin) = [sem(n) for n in (
             "block_chosen", "block_gates", "gathered", "x_high", "x_low", "w_high", "w_low",
             "unit_multiplied", "chunk_evacuated", "hidden_transposed", "bias_added", "clamped",
             "sigmoid_ready", "gated_ready", "act_ready", "act_high", "act_low", "block_gatesT",
             "block_gatesT_ready", "combined", "columns_copied", "linear_clamped")]
        dve_seq, act_seq, pool_seq = sem("dve_seq"), sem("act_seq"), sem("pool_seq")
        y_all, y_sum, rms3, y_ok, y_out, n2T_dve, msk_ok = [sem(n) for n in (
            "experts_done", "y_sum", "rms3", "y_ready", "y_stored", "n2T_by_dve", "masks_ready")]

        def slot_of(j):
            return (N_FRONT + j) % SLOTS

        def filled(eng, n, j):
            eng.wait_ge(full[slot_of(j)], 16 * (n + (N_FRONT + j) // SLOTS + 1))

        def level_views(ap, hh):
            a = ap.rearrange("p h (n two j) -> p h n two j", two=2, j=hh)
            return a[:, :, :, 0, :], a[:, :, :, 1, :]

        steps = [(d, hh) for d in (0, 1) for hh in [P] + LEVELS]
        N_STEP = len(steps)
        block = keep.enter_context(nc.Block())

        @block.sync
        def _(sp):
            sp.dma_start(h[:], x_v).then_inc(x_in, 16)
            for i, col in enumerate(W_IN_COLUMNS):
                if i >= SLOTS:
                    sp.wait_ge(proj, i - SLOTS + 1)
                sp.dma_start(ring[:, i % SLOTS], w_in_v[:, :, col * CW:(col + 1) * CW])\
                  .then_inc(full[i % SLOTS], 16)
            for i in range(2):
                sp.wait_ge(proj, N_IN + i - SLOTS + 1)
                sp.dma_start(ring[:, (N_IN + i) % SLOTS], w_out_v[:, :, i * CW:(i + 1) * CW])\
                  .then_inc(full[(N_IN + i) % SLOTS], 16)

            def expert_chunk(e, j):
                if j < 4:
                    lo = (j // 2) * CW + (j % 2) * D
                    src = w1_v[e, :, :, lo:lo + CW]
                else:
                    src = w2_v[e, :, :, (j - 4) * CW:(j - 3) * CW]
                sp.dma_start(ring[:, slot_of(j)], src).then_inc(full[slot_of(j)], 16)

            def block_chunks(n, e):
                for j in range(N_EXP):
                    sp.wait_ge(s_wl, UNITS * (n - 1) + DONE[j])
                    expert_chunk(e, j)

            for j in range(N_EXP):
                if j < 4:
                    sp.wait_ge(proj, j + 4)
                else:
                    sp.wait_ge(wout_done, 1)
                expert_chunk(0, j)
            with sp.Fori(1, E) as e:
                block_chunks(e, e)
            sp.wait_ge(routed, 1)
            n_more = sp.value_load(nextra[0:1, 0:1], min_val=0, max_val=EXTRA)
            with sp.Fori(0, EXTRA) as i:
                with sp.If(i < n_more):
                    e = sp.value_load(table[0:1, 0, bass.ds(i, 1)], min_val=0, max_val=E - 1)
                    block_chunks(E + i, e)
                sp.nop()
            sp.wait_ge(y_ok, 1)
            sp.dma_start(out_v[:, 0, :], h[:, 0, :]).then_inc(y_out, 16)
            sp.wait_ge(y_ok, 2)
            sp.dma_start(out_v[:, 1, :], h[:, 1, :]).then_inc(y_out, 16)
            sp.wait_ge(y_out, 32)

        @block.gpsimd
        def _(pool):
            g = nc.gpsimd
            g.memset(eps[:], EPS).then_inc(fills, 1)
            g.memset(ones[:], 1.0).then_inc(fills, 1)
            g.memset(ones_v[:], 1.0 / P).then_inc(fills, 1)
            g.memset(ones_c[:], 1.0 / CW).then_inc(fills, 1)
            g.memset(bb[:, :, 0:1], 0.0).then_inc(fills, 1)
            g.memset(am[:], 0.0).then_inc(fills, 1)
            pool.wait_ge(prm_sb, 3)
            g.memset(u[:, :, 0:PAD], 0.0).then_inc(fills, 1)
            g.memset(u[:, :, PAD + T:], 0.0).then_inc(fills, 1)
            pool.wait_ge(m_in, 16)
            g.tensor_copy(msk[:], msk_f).then_inc(msk_ok, 1)
            for k, (d, hh) in enumerate(steps):
                pool.wait_ge(exp_ok, k + 1)
                if k in (0, 8):
                    pool.wait_ge(f_ok, 2 + 2 * (k // 8))
                if k == 0:
                    pool.wait_ge(ev_dve, 2)
                if k >= 2:
                    pool.wait_ge(prod, k - 1)
                (ea, eb_), (wa, wb) = level_views(ex[:, k % 2], hh), level_views(wk[:, k % 2], hh)
                (qa, qb), (ka, kb_) = level_views(q[:], hh), level_views((kf, kb)[d][:], hh)
                first, second = (ka, qb) if d == 0 else (qa, kb_)
                g.tensor_tensor(wa, first, ea, ALU.mult)
                g.tensor_tensor(wb, second, eb_, ALU.mult).then_inc(w_ok, 1)
            pool.wait_ge(prod, N_STEP - 1)
            g.tensor_tensor(wk[:, 0], kf[:], kb[:], ALU.add).then_inc(w_ok, 1)

            def choose_gates(n, e):
                g.tensor_copy(cur[:, 1, :], gates[:, :, bass.ds(e, 1)].rearrange("p a b -> p (a b)"))\
                 .then_inc(s_cur, 1)
                if not (isinstance(n, int) and n == 0):
                    pool.wait_ge(s_gps, n)
                pool.wait_ge(s_cur, n + 1)
                pool.wait_ge(s_sel, n + 1)
                for t in range(NT):
                    last = g.tensor_tensor(selg[:, t], sel[:, t:t + 1, :].to_broadcast([P, 2, BLK]),
                                           cur[:, 1, t:t + 1].unsqueeze(2).to_broadcast([P, 2, BLK]), ALU.mult)
                last.then_inc(s_selg, 1)

            def gated(n, hf):
                pool.wait_ge(s_glu, 2 * n + hf + 1)
                pool.wait_ge(s_sig, 2 * n + hf + 1)
                g.tensor_tensor(gs[:], glu[:], sig[:], ALU.mult).then_inc(s_gs, 1)

            def body(n, e):
                choose_gates(n, e)
                gated(n, 0)
                gated(n, 1)

            pool.wait_ge(routed, 1)
            body(0, 0)
            with pool.Fori(1, E) as e:
                body(e, e)
            n_more = pool.value_load(nextra[0:1, 0:1], min_val=0, max_val=EXTRA)
            with pool.Fori(0, EXTRA) as i:
                with pool.If(i < n_more):
                    e = pool.value_load(table[0:1, 0, bass.ds(i, 1)], min_val=0, max_val=E - 1)
                    body(E + i, e)
                pool.nop()

        @block.scalar
        def _(act):
            a = nc.scalar
            act.dma_start(cst[:], consts).then_inc(c_in, 16)
            act.dma_start(rows[0:TAPS * CH, 0, :], dww).then_inc(p_in, 16)
            act.dma_start(rows[0:PRM, 1, :], prm).then_inc(p_in, 16)
            act.dma_start(b1_rows, b1).then_inc(b1_in, 16)
            act.dma_start(msk_f, masks).then_inc(m_in, 16)
            act.dma_start(wrow[:], norm2_w.partition_broadcast(P)).then_inc(w2r_in, 16)
            act.dma_start(rw[:], router_w.rearrange("(c p) e -> p c e", p=P)).then_inc(r_in, 16)
            act.dma_start(rb[:], router_b.rearrange("(a e) -> a e", a=1)).then_inc(r_in, 16)

            step = [0]

            def link(ins):
                step[0] += 1
                ins.then_inc(act_seq, 1)
                act.wait_ge(act_seq, step[0])

            act.wait_ge(fills, 1)
            act.wait_ge(x_in, 16)
            for t in range(NT):
                last = a.activation(wk[:, 0:2].rearrange("p a h t -> p a (h t)")[:, t], h[:, t, :], ACT.Square,
                                    accum_out=ssum[:, t:t + 1])
            link(last)
            a.activation(ssum[:, 2:4], ssum[:, 0:2], ACT.Sqrt, bias=eps[:], scale=1.0 / D).then_inc(rms1, 1)
            act.wait_ge(prm_sb, 2)
            for c in range(C // 2):
                act.wait_ge(xT_ok, c // 2 + 1)
                a.activation(nT[:, c, :], ps[:, 4 + c // 2, (c % 2) * T:(c % 2 + 1) * T], ACT.Copy, scale=n1w[:, c:c + 1])\
                 .then_inc(nT_act, 1)
            act.wait_ge(sc_ok, 1)
            a.activation(lbs[:, 2:4], lbs[:, 0:2], ACT.Exp).then_inc(sc_ok, 1)

            act.wait_ge(prm_sb, 3)
            act.wait_ge(proj, CV + 1)
            a.activation(cv[:], heads(pair(0)), ACT.Copy).then_inc(ev_act, 1)
            act.wait_ge(proj, CG + 1)
            a.activation(sA, heads(pair(1)), ACT.Sigmoid).then_inc(ev_act, 1)
            act.wait_ge(proj, FF + 1)
            a.activation(sB, heads(pair(0)), ACT.Sigmoid).then_inc(ev_act, 1)
            act.wait_ge(f_ok, 2)
            a.activation(sB, sB, ACT.Ln).then_inc(logf_ok, 1)
            act.wait_ge(proj, QZ + 1)
            act.wait_ge(ev_dve, 1)
            a.activation(sA, heads(pair(1)), ACT.Sigmoid).then_inc(ev_act, 1)
            act.dma_start(b2_rows, b2).then_inc(b2_in, 16)

            def exps(k):
                act.wait_ge(e_ok, k + 1)
                a.activation(ex[:, k % 2], ex[:, k % 2], ACT.Exp).then_inc(exp_ok, 1)

            exps(0)
            exps(1)
            act.wait_ge(proj, FB + 1)
            act.wait_ge(sc_ok, 3)
            a.activation(sB, heads(pair(0)), ACT.Sigmoid).then_inc(ev_act, 1)
            act.wait_ge(f_ok, 4)
            a.activation(sB, sB, ACT.Ln).then_inc(logf_ok, 1)
            for k in range(2, 4):
                exps(k)
            act.wait_ge(proj, IV + 1)
            a.activation(v[:], pair(1).rearrange("p (t e) -> p t e", t=NT), ACT.Copy).then_inc(ev_act, 1)
            for k in range(4, 8):
                exps(k)
            act.wait_ge(proj, GZ + 1)
            act.wait_ge(ev_dve, 2)
            a.activation(sA, heads(pair(0)), ACT.Sigmoid).then_inc(ev_act, 1)
            for k in range(8, 10):
                exps(k)
            act.wait_ge(xc_ok, 1)
            a.activation(u[:, :, 0:T], acc[:], ACT.Square).then_inc(xc2_ok, 1)
            for k in range(10, N_STEP):
                exps(k)
            act.wait_ge(var_ps, 1)
            a.activation(u[:, 0, 0:T], ps[:, 3, T:2 * T], ACT.Sqrt, bias=eps[:]).then_inc(std_ok, 1)
            act.wait_ge(ln_ok, 1)
            for c in range(CH):
                last = a.activation(u[:, c, 0:T], acc[:, c, :], ACT.Sigmoid,
                                    scale=prmT[:, 20 + c:21 + c], bias=prmT[:, 24 + c:25 + c])
            last.then_inc(lsg_ok, 1)
            act.wait_ge(av, 1)
            act.wait_ge(lev, N_STEP + 1)
            a.activation(wk[:, 1], heads(pair(0)), ACT.Square).then_inc(o2_ok, 1)
            act.wait_ge(oms_ps, 1)
            a.activation(ex[:, 0], heads(pair(3)), ACT.Sqrt, bias=eps[:]).then_inc(ostd_ok, 1)
            for t in range(NT):
                act.wait_ge(h_ok, t + 1)
                last = a.activation(ex[:, 0:2].rearrange("p a h t -> p a (h t)")[:, t], h[:, t, :], ACT.Square,
                                    accum_out=ssum[:, t:t + 1])
            link(last)
            a.activation(ssum[:, 2:4], ssum[:, 0:2], ACT.Sqrt, bias=eps[:], scale=1.0 / D).then_inc(rms2, 1)
            act.wait_ge(n2_ok, NT)
            act.dma_start(wrow[:], final_w.partition_broadcast(P)).then_inc(fw_in, 16)
            for i in range(2):
                act.wait_ge(n2T_ps, i + 1)
                a.activation(nT[:, 2 * i:2 * i + 2, :], ps[:, i, :].rearrange("p (c t) -> p c t", c=2), ACT.Copy)\
                 .then_inc(n2T_sb, 1)
            act.wait_ge(lg_ok, 1)
            for t in range(NT):
                last = a.activation(rt[:, 0, t, :], lg[:, t, :], ACT.Exp, bias=sm[:, 0, t:t + 1])
            last.then_inc(ex4_ok, 1)
            act.wait_ge(gT_ps, 1)
            a.activation(gT, ps[0:E, 2, T:2 * T], ACT.Copy).then_inc(gT_sb, 1)

            def split_high(n, uu):
                j, half = ORDER[uu]
                if half == 0:
                    filled(act, n, j)
                if not (isinstance(n, int) and UNITS * n + uu < WD):
                    act.wait_ge(s_mm, UNITS * n + uu + 1 - WD)
                a.activation(wh[:, uu % WD], ring[:, slot_of(j), 4 * half:4 * half + 4, :], ACT.Copy)\
                 .then_inc(s_wh, 1)

            def evacuate(n, j):
                act.wait_ge(s_mm, UNITS * n + DONE[j])
                if j < 4:
                    if j >= 2:
                        act.wait_ge(s_tr, 4 * n + j - 1)
                    dst = hid[:, j % 2, :]
                else:
                    dst = y[:, (j - 4) * CW:(j - 3) * CW]
                a.activation(dst, ps[:, j % 2, :], ACT.Copy).then_inc(s_ev, 1)

            def x_high(n):
                act.wait_ge(s_xps, n + 1)
                if not (isinstance(n, int) and n == 0):
                    act.wait_ge(s_mm, UNITS * (n - 1) + DONE[3])
                a.activation(xg[:, :, 0:BLK], ps[:, 3, :].rearrange("p (c s) -> p c s", c=C), ACT.Copy)\
                 .then_inc(s_xh, 1)

            def gates_out(n):
                act.wait_ge(s_gps, n + 1)
                a.activation(gsel[:], ps[:, 3, 0:T].rearrange("p (i t) -> p i t", i=NT), ACT.Copy).then_inc(s_gt, 1)

            def sigmoid(n, hf):
                act.wait_ge(s_glu, 2 * n + hf + 1)
                a.activation(sig[:], glu[:], ACT.Sigmoid, scale=ALPHA).then_inc(s_sig, 1)

            def a_high(n, hf):
                act.wait_ge(s_act, 2 * n + hf + 1)
                a.activation(aT[:, 4 * hf:4 * hf + 4, 0:BLK], act_[:], ACT.Copy).then_inc(s_ah, 1)

            def y_out_of(n, j):
                if not (isinstance(n, int) and n == 0) and j == 4:
                    act.wait_ge(s_comb, NPC * n)
                evacuate(n, j)

            def body(n, before, following):
                for uu in range(UNITS):
                    split_high(n, uu)
                    if uu < 2 and before:
                        y_out_of(n - 1, 4 + uu)
                    if uu == 3:
                        evacuate(n, 0)
                    if uu == 4 and before:
                        gates_out(n - 1)
                    if uu == 5:
                        evacuate(n, 1)
                    if uu == 7:
                        evacuate(n, 2)
                    if uu == 8:
                        sigmoid(n, 0)
                    if uu == 9:
                        a_high(n, 0)
                        evacuate(n, 3)
                    if uu == 10:
                        sigmoid(n, 1)
                        if following:
                            x_high(n + 1)
                        a_high(n, 1)

            def finish(n):
                y_out_of(n, 4)
                y_out_of(n, 5)
                gates_out(n)

            act.wait_ge(routed, 1)
            act.wait_ge(acc0, 1)
            x_high(0)
            body(0, False, True)
            with act.Fori(1, E - 1) as n:
                body(n, True, True)
            body(E - 1, True, False)
            finish(E - 1)
            n_more = act.value_load(nextra[0:1, 0:1], min_val=0, max_val=EXTRA)
            with act.Fori(0, EXTRA) as i:
                with act.If(i < n_more):
                    x_high(E + i)
                    body(E + i, False, False)
                    finish(E + i)
                act.nop()
            for t in range(NT):
                act.wait_ge(y_sum, t + 1)
                last = a.activation(n2[:, t, :], h[:, t, :], ACT.Square, accum_out=ssum[:, t:t + 1])
            link(last)
            a.activation(ssum[:, 2:4], ssum[:, 0:2], ACT.Sqrt, bias=eps[:], scale=1.0 / D).then_inc(rms3, 1)

        @block.vector
        def _(dve):
            w = nc.vector
            step = [0]

            def link(ins):
                step[0] += 1
                ins.then_inc(dve_seq, 1)
                dve.wait_ge(dve_seq, step[0])

            dve.wait_ge(rms1, 1)
            link(w.reciprocal(ssum[:, 4:6], ssum[:, 2:4]))
            for t in range(NT):
                w.tensor_scalar(n2[:, t, :], h[:, t, :], ssum[:, 4 + t:5 + t], None, ALU.mult).then_inc(xn_ok, 1)
            dve.wait_ge(prm_ps, 1)
            w.tensor_copy(dwT[:], ps[:, 0, 0:TAPS * CH])
            w.tensor_copy(prmT[:], ps[:, 0, P:P + PRM]).then_inc(prm_sb, 2)
            dve.wait_ge(prm_sb, 2)
            for c in range(C // 2, C):
                dve.wait_ge(xT_ok, c // 2 + 1)
                w.tensor_scalar(nT[:, c, :], ps[:, 4 + c // 2, (c % 2) * T:(c % 2 + 1) * T], n1w[:, c:c + 1], None, ALU.mult)\
                 .then_inc(nT_dve, 1)
            dve.wait_ge(prm_ps, 2)
            w.tensor_copy(b1T[:], ps[:, 1, :].rearrange("p (c e) -> p c e", e=E)).then_inc(prm_sb, 1)
            dve.wait_ge(prm_sb, 3)
            lbv = prmT[:, 0:16].rearrange("p (d r h) -> p r d h", d=2, r=2)
            link(w.tensor_tensor(lbs[:, 4], lbv[:, 0], lbv[:, 1], ALU.max))
            w.tensor_tensor(lbs[:, 0], lbv[:, 0], lbs[:, 4], ALU.subtract)
            w.tensor_tensor(lbs[:, 1], lbv[:, 1], lbs[:, 4], ALU.subtract).then_inc(sc_ok, 1)
            dve.wait_ge(sc_ok, 2)
            link(w.tensor_tensor(lbs[:, 4], lbs[:, 2], lbs[:, 3], ALU.add))
            link(w.reciprocal(lbs[:, 5], lbs[:, 4]))
            link(w.tensor_tensor(lbs[:, 0], lbs[:, 2], lbs[:, 5], ALU.mult))
            link(w.tensor_scalar(lbs[:, 1], lbs[:, 0], -1.0, 1.0, ALU.mult, ALU.add))
            dve.wait_ge(ev_act, 2)
            dve.wait_ge(fills, 8)
            w.tensor_tensor(u[:, :, PAD:PAD + T], cv[:], sA, ALU.mult).then_inc(ev_dve, 1)
            dve.wait_ge(ev_dve, 1)

            conv_step = [0]

            def conv(lo, hi):
                for tap in range(lo, hi):
                    for c in range(CH):
                        wt = dwT[:, tap * CH + c:tap * CH + c + 1]
                        if tap == 0:
                            ins = w.tensor_scalar(acc[:, c, :], u[:, c, 0:T], wt, prmT[:, 16 + c:17 + c],
                                                  ALU.mult, ALU.add)
                        else:
                            dve.wait_ge(conv_ok, (tap - 1) * CH + c + 1)
                            ins = w.scalar_tensor_tensor(out=acc[:, c, :], in0=u[:, c, tap:tap + T], scalar=wt,
                                                         in1=acc[:, c, :], op0=ALU.mult, op1=ALU.add)
                        ins.then_inc(conv_ok, 1)

            def gates_of(d):
                dve.wait_ge(ev_act, (3, 5)[d])
                for hd in range(H):
                    last = w.tensor_scalar(sB[:, hd, :], sB[:, hd, :], lbs[:, 1, d, hd:hd + 1],
                                           lbs[:, 0, d, hd:hd + 1], ALU.mult, ALU.add)
                last.then_inc(f_ok, 1)
                dve.wait_ge(f_ok, 2 * d + 1)
                w.tensor_scalar((kf, kb)[d][:], sB, -1.0, 1.0, ALU.mult, ALU.add).then_inc(f_ok, 1)

            def prefix(d):
                dve.wait_ge(logf_ok, d + 1)
                for hd in range(H):
                    dst = bf[:, hd, :] if d == 0 else bb[:, hd, 1:T + 1]
                    last = w.tensor_tensor_scan(dst, ones[:], sB[:, hd, :], 0.0, ALU.mult, ALU.add)
                last.then_inc(sc_ok, 1)
                dve.wait_ge(sc_ok, 3 + d)

            def exponents(k):
                d, hh = steps[k]
                b = bf[:] if d == 0 else bb[:, :, 0:T]
                if k >= 2:
                    dve.wait_ge(w_ok, k - 1)
                first, second = level_views(b, hh)
                ea, eb_ = level_views(ex[:, k % 2], hh)
                mid = first[:, :, :, hh - 1:hh] if d == 0 else second[:, :, :, 0:1]
                mid = mid.to_broadcast([P, H, T // (2 * hh), hh])
                w.tensor_tensor(ea, mid, first, ALU.subtract)
                w.tensor_tensor(eb_, second, mid, ALU.subtract).then_inc(e_ok, 1)

            def merge(k):
                dve.wait_ge(prod, k + 1)
                if k < N_STEP and steps[k][1] == P:
                    w.tensor_copy(off[:, steps[k][0]], ps[:, 4 + 2 * (k % 2), :].rearrange("p (h t) -> p h t", h=H))\
                     .then_inc(lev, 1)
                    return
                if k < N_STEP:
                    m = len(LEVELS) * steps[k][0] + LEVELS.index(steps[k][1])
                else:
                    m = 2 * len(LEVELS)
                dve.wait_ge(lev, k)
                mk = msk[:, m:m + 1, :].to_broadcast([P, H * NT, P])
                w.copy_predicated(am[:].rearrange("p h i t -> p (h i) t"), mk,
                                  pair(2 + k % 2).rearrange("p (a t) -> p a t", t=P)).then_inc(lev, 1)

            conv(0, 8)
            gates_of(0)
            conv(8, 16)
            prefix(0)
            dve.wait_ge(msk_ok, 1)
            exponents(0)
            exponents(1)
            dve.wait_ge(ev_act, 4)
            w.tensor_tensor(q[:], heads(pair(1)), sA, ALU.mult).then_inc(ev_dve, 1)
            conv(16, TAPS)
            gates_of(1)
            for k in range(0, 6):
                exponents(k + 2)
                merge(k)
            prefix(1)
            exponents(8)
            merge(6)
            exponents(9)
            merge(7)
            dve.wait_ge(ev_act, 7)
            w.tensor_tensor(gate[:], heads(pair(0)), sA, ALU.mult).then_inc(ev_dve, 1)
            dve.wait_ge(mu_ps, 1)
            w.tensor_tensor(acc[:], acc[:], ps[:, 3:4, 0:T].to_broadcast([P, CH, T]), ALU.subtract)\
             .then_inc(xc_ok, 1)
            for k in range(8, N_STEP - 2):
                exponents(k + 2)
                merge(k)
            dve.wait_ge(std_ok, 1)
            w.reciprocal(u[:, 1, 0:T], u[:, 0, 0:T]).then_inc(dve_seq, 1)
            step[0] += 1
            merge(N_STEP - 2)
            merge(N_STEP - 1)
            dve.wait_ge(dve_seq, step[0])
            w.tensor_tensor(acc[:], acc[:], u[:, 1:2, 0:T].to_broadcast([P, CH, T]), ALU.mult).then_inc(ln_ok, 1)
            merge(N_STEP)
            dve.wait_ge(lsg_ok, 1)
            dve.wait_ge(ln_ok, 1)
            for c in range(CH):
                last = w.tensor_scalar(acc[:, c, :], acc[:, c, :], prmT[:, 20 + c:21 + c], prmT[:, 24 + c:25 + c],
                                       ALU.mult, ALU.add)
            link(last)
            w.tensor_tensor(cat[:, 4:8, :], acc[:], u[:, :, 0:T], ALU.mult).then_inc(catb_ok, 1)
            dve.wait_ge(ostd_ok, 1)
            link(w.reciprocal(ex[:, 1], ex[:, 0]))
            link(w.tensor_tensor(wk[:, 0], heads(pair(0)), ex[:, 1], ALU.mult))
            for hd in range(H):
                last = w.scalar_tensor_tensor(out=cat[:, hd, :], in0=wk[:, 0, hd, :], scalar=prmT[:, 28 + hd:29 + hd],
                                              in1=gate[:, hd, :], op0=ALU.mult, op1=ALU.mult)
            last.then_inc(cata_ok, 1)
            for t in range(NT):
                for half in range(2):
                    dve.wait_ge(oproj, 2 * t + half + 1)
                    cols = slice(half * CW, (half + 1) * CW)
                    last = w.tensor_tensor(h[:, t, cols], h[:, t, cols], ps[:, (4, 2)[half] + t, :], ALU.add)
                last.then_inc(h_ok, 1)
            dve.wait_ge(rms2, 1)
            dve.wait_ge(w2r_in, 16)
            link(w.reciprocal(ssum[:, 4:6], ssum[:, 2:4]))
            for t in range(NT):
                w.scalar_tensor_tensor(out=n2[:, t, :], in0=h[:, t, :], scalar=ssum[:, 4 + t:5 + t], in1=wrow[:],
                                       op0=ALU.mult, op1=ALU.mult).then_inc(n2_ok, 1)
            for i in range(2, 4):
                dve.wait_ge(n2T_ps, i + 1)
                w.tensor_copy(nT[:, 2 * i:2 * i + 2, :], ps[:, 4 + i, :].rearrange("p (c t) -> p c t", c=2))\
                 .then_inc(n2T_dve, 1)
            dve.wait_ge(lgt_ps, 1)
            link(w.tensor_copy(lg[:], ps[:, 3, 0:NT * E].rearrange("p (i e) -> p i e", i=NT)))
            for t in range(NT):
                last = w.max(mx[:, t, :], lg[:, t, :])
            link(last)
            w.tensor_scalar(sm[:, 0, :], mx[:, :, 0], -1.0, None, ALU.mult).then_inc(lg_ok, 1)
            v4 = mx[:, :, TOPK - 1:TOPK].to_broadcast([P, NT, E])
            w.tensor_tensor(rt[:, 1], lg[:], v4, ALU.is_gt)
            link(w.tensor_tensor(rt[:, 2], lg[:], v4, ALU.is_equal))
            w.tensor_reduce(sm[:, 1, :], rt[:, 1], AX.X, ALU.add)
            for t in range(NT):
                last = w.tensor_tensor_scan(rt[:, 3, t, :], ones[:, 0:E], rt[:, 2, t, :], 0.0, ALU.mult, ALU.add)
            link(last)
            link(w.tensor_tensor(rt[:, 4], rt[:, 3], sm[:, 1, :].unsqueeze(2).to_broadcast([P, NT, E]), ALU.add))
            link(w.tensor_scalar(rt[:, 5], rt[:, 4], float(TOPK), None, ALU.is_le))
            link(w.tensor_tensor(rt[:, 6], rt[:, 5], rt[:, 2], ALU.mult))
            w.tensor_tensor(rt[:, 7], rt[:, 6], rt[:, 1], ALU.add).then_inc(sel_ok, 1)
            dve.wait_ge(sel_ok, 1)
            dve.wait_ge(ex4_ok, 1)
            link(w.tensor_tensor(rt[:, 1], rt[:, 0], rt[:, 7], ALU.mult))
            link(w.tensor_reduce(sm[:, 2, :], rt[:, 1], AX.X, ALU.add))
            link(w.reciprocal(sm[:, 3, :], sm[:, 2, :]))
            w.tensor_tensor(gates[:], rt[:, 1], sm[:, 3, :].unsqueeze(2).to_broadcast([P, NT, E]), ALU.mult)\
             .then_inc(gates_ok, 1)
            dve.wait_ge(rank_ps, 1)
            link(w.scalar_tensor_tensor(out=rt[:, 2], in0=ps[:, 3, 64:64 + NT * E].rearrange("p (i e) -> p i e", i=NT),
                                        scalar=1.0, in1=rt[:, 7], op0=ALU.add, op1=ALU.mult))
            w.tensor_scalar(rankm[:], rt[:, 2], 1.0, None, ALU.subtract)
            link(w.tensor_copy(ctf[0:1, 0, :], ps[0:1, 3, P:P + E]))
            link(w.tensor_scalar(ctf[0:1, 1, :], ctf[0:1, 0, :], float(BLK), None, ALU.is_gt))
            for k in range(2, T // BLK):
                link(w.scalar_tensor_tensor(out=ctf[0:1, 1, :], in0=ctf[0:1, 0, :], scalar=float(k * BLK),
                                            in1=ctf[0:1, 1, :], op0=ALU.is_gt, op1=ALU.add))
            link(w.tensor_tensor_scan(ctf[0:1, 2, :], ones[0:1, 0:E], ctf[0:1, 1, :], 0.0, ALU.mult, ALU.add))
            jj = iota[0:1, 0:EXTRA].unsqueeze(2).to_broadcast([1, EXTRA, E])
            link(w.tensor_tensor(cmp_[0:1, 0], ctf[0:1, 2:3, :].to_broadcast([1, EXTRA, E]), jj, ALU.is_le))
            link(w.tensor_tensor(cmp_[0:1, 1], ctf[0:1, 1:2, :].to_broadcast([1, EXTRA, E]), cmp_[0:1, 0], ALU.mult))
            w.tensor_reduce(eb[0:1, 0, 0:EXTRA], cmp_[0:1, 0], AX.X, ALU.add)
            link(w.tensor_reduce(eb[0:1, 1, 0:EXTRA], cmp_[0:1, 1], AX.X, ALU.add))
            link(w.tensor_tensor(eb[0:1, 2, 0:EXTRA], iota[0:1, 0:EXTRA], eb[0:1, 1, 0:EXTRA], ALU.subtract))
            link(w.tensor_scalar(eb[0:1, 3, 0:EXTRA], eb[0:1, 2, 0:EXTRA], float(BLK), float(BLK), ALU.mult, ALU.add))
            w.tensor_scalar(table[0:1, 0, 0:EXTRA], eb[0:1, 0, 0:EXTRA], float(E - 1), None, ALU.min)
            w.tensor_scalar(table[0:1, 1, 0:EXTRA], eb[0:1, 3, 0:EXTRA], float(T - BLK), None, ALU.min)
            w.tensor_copy(nextra[:], ctf[0:1, 2, E - 1:E]).then_inc(routed, 1)

            def split_low(n, uu):
                dve.wait_ge(s_wh, UNITS * n + uu + 1)
                if not (isinstance(n, int) and UNITS * n + uu < WD):
                    dve.wait_ge(s_mm, UNITS * n + uu + 1 - WD)
                j, half = ORDER[uu]
                w.tensor_tensor(wl[:, uu % WD], ring[:, slot_of(j), 4 * half:4 * half + 4, :],
                                wh[:, uu % WD].bitcast(F32), ALU.subtract).then_inc(s_wl, 1)

            def x_low(n):
                dve.wait_ge(s_xh, n + 1)
                w.tensor_tensor(xg[:, :, BLK:2 * BLK], ps[:, 3, :].rearrange("p (c s) -> p c s", c=C),
                                xg[:, :, 0:BLK].bitcast(F32), ALU.subtract).then_inc(s_xl, 1)

            def choose(n, e, r):
                if not (isinstance(n, int) and n == 0):
                    dve.wait_ge(s_xps, n)
                    dve.wait_ge(s_selg, n)
                for t in range(NT):
                    last = w.tensor_scalar(sel[:, t, :], iota[:, bass.ds(r, BLK)],
                                           rankm[:, t, bass.ds(e, 1)], None, ALU.is_equal)
                last.then_inc(s_sel, 1)

            def add_bias(n, e, hf):
                dve.wait_ge(s_tr, 4 * n + 2 * hf + 2)
                if not (isinstance(n, int) and n == 0 and hf == 0):
                    dve.wait_ge(s_lin, 2 * n + hf)
                bias = b1T[:, :, bass.ds(e, 1)].rearrange("p (g c) o -> p g c o", g=2)[:, :, 4 * hf:4 * hf + 4, :]
                w.tensor_tensor(pre[:], ps[:, 2, :].rearrange("p (g c s) -> p g c s", g=2, c=4),
                                bias.to_broadcast([P, 2, 4, BLK]), ALU.add).then_inc(s_pre, 1)
                dve.wait_ge(s_pre, 2 * n + hf + 1)
                if not (isinstance(n, int) and n == 0 and hf == 0):
                    dve.wait_ge(s_gs, 2 * n + hf)
                w.tensor_scalar(glu[:], pre[:, 0], LIMIT, None, ALU.min).then_inc(s_glu, 1)
                w.tensor_scalar(lin[:], pre[:, 1], LIMIT, -LIMIT, ALU.min, ALU.max).then_inc(s_lin, 1)

            def activate(n, hf):
                dve.wait_ge(s_gs, 2 * n + hf + 1)
                dve.wait_ge(s_lin, 2 * n + hf + 1)
                if not (isinstance(n, int) and n == 0 and hf == 0):
                    dve.wait_ge(s_al, 2 * n + hf)
                w.scalar_tensor_tensor(out=act_[:], in0=lin[:], scalar=1.0, in1=gs[:], op0=ALU.add, op1=ALU.mult)\
                 .then_inc(s_act, 1)

            def a_low(n, hf):
                dve.wait_ge(s_ah, 2 * n + hf + 1)
                w.tensor_tensor(aT[:, 4 * hf:4 * hf + 4, BLK:2 * BLK], act_[:],
                                aT[:, 4 * hf:4 * hf + 4, 0:BLK].bitcast(F32), ALU.subtract).then_inc(s_al, 1)

            def body(n, e, following):
                for uu in range(UNITS):
                    split_low(n, uu)
                    if uu == 4 and following:
                        choose(n + 1, e + 1, 0)
                    if uu == 6:
                        add_bias(n, e, 0)
                    if uu == 8:
                        activate(n, 0)
                    if uu == 9:
                        a_low(n, 0)
                        add_bias(n, e, 1)
                    if uu == 10:
                        activate(n, 1)
                        a_low(n, 1)
                    if uu == 11 and following:
                        x_low(n + 1)

            choose(0, 0, 0)
            x_low(0)
            body(0, 0, True)
            with dve.Fori(1, E - 1) as n:
                body(n, n, True)
            body(E - 1, E - 1, False)
            n_more = dve.value_load(nextra[0:1, 0:1], min_val=0, max_val=EXTRA)
            with dve.Fori(0, EXTRA) as i:
                with dve.If(i < n_more):
                    e = dve.value_load(table[0:1, 0, bass.ds(i, 1)], min_val=0, max_val=E - 1)
                    r = dve.value_load(table[0:1, 1, bass.ds(i, 1)], min_val=0, max_val=T - BLK)
                    choose(E + i, e, r)
                    x_low(E + i)
                    body(E + i, e, False)
                dve.nop()
            dve.wait_ge(y_all, 1)
            for t in range(NT):
                w.tensor_tensor(h[:, t, :], h[:, t, :], ps[:, 4 + 2 * t:6 + 2 * t, :].rearrange("p a b -> p (a b)"),
                                ALU.add).then_inc(y_sum, 1)
            dve.wait_ge(rms3, 1)
            dve.wait_ge(fw_in, 16)
            link(w.reciprocal(ssum[:, 4:6], ssum[:, 2:4]))
            for t in range(NT):
                w.scalar_tensor_tensor(out=h[:, t, :], in0=h[:, t, :], scalar=ssum[:, 4 + t:5 + t], in1=wrow[:],
                                       op0=ALU.mult, op1=ALU.mult).then_inc(y_ok, 1)

        @block.tensor
        def _(pe):
            mm, tr = nc.tensor.matmul, nc.tensor.transpose
            pe.wait_ge(c_in, 16)
            pe.wait_ge(p_in, 32)
            tr(ps[:, 0, 0:TAPS * CH], rows[0:TAPS * CH, 0, :], ident[0:TAPS * CH, 0:TAPS * CH])
            tr(ps[:, 0, P:P + PRM], rows[0:PRM, 1, :], ident[0:PRM, 0:PRM]).then_inc(prm_ps, 1)
            pe.wait_ge(b1_in, 16)
            for c in range(2 * C):
                last = tr(ps[:, 1, c * E:(c + 1) * E], b1_rows[:, c * P:(c + 1) * P], ident[0:E, 0:E])
            last.then_inc(prm_ps, 1)
            pe.wait_ge(xn_ok, NT)
            for c in range(C):
                for t in range(NT):
                    last = tr(ps[:, 4 + c // 2, (c % 2) * T + t * P:(c % 2) * T + (t + 1) * P],
                              n2[:, t, c * P:(c + 1) * P], ident)
                if c % 2:
                    last.then_inc(xT_ok, 1)
            pe.wait_ge(nT_act, C // 2)
            pe.wait_ge(nT_dve, C // 2)
            pe.wait_ge(prm_sb, 3)

            def project_part(i, part):
                wt = ring[:, i % SLOTS]
                base = 2 * (i % 2)
                for c in range(C):
                    if i == IV:
                        last = mm(ps[:, base + part, :], nT[:, c, part * P:(part + 1) * P], wt[:, c, :],
                                  start=(c == 0), stop=(c == C - 1))
                    else:
                        o = (part % 2) * T
                        last = mm(ps[:, base + part // 2, o:o + T], wt[:, c, part * P:(part + 1) * P],
                                  nT[:, c, :], start=(c == 0), stop=(c == C - 1))
                return last

            def begin(i):
                pe.wait_ge(full[i % SLOTS], 16 * (i // SLOTS + 1))
                if i >= 2:
                    pe.wait_ge(ev_act, (1, 2, 3, 4, 5)[i - 2])
                    if i - 2 == QZ:
                        pe.wait_ge(ev_dve, 2)

            def products(k):
                pe.wait_ge(w_ok, k + 1)
                if k >= 2:
                    pe.wait_ge(lev, k - 1)
                s = wk[:, k % 2]
                for hd in range(H):
                    if k < N_STEP and steps[k][1] == P:
                        d = steps[k][0]
                        last = mm(ps[:, 4 + 2 * (k % 2), hd * P:(hd + 1) * P], s[:, hd, d * P:(d + 1) * P],
                                  s[:, hd, (1 - d) * P:(2 - d) * P], start=True, stop=True)
                        continue
                    for t in range(NT):
                        a = hd * NT + t
                        tile = slice(t * P, (t + 1) * P)
                        rhs = s[:, hd, tile] if k < N_STEP else q[:, hd, tile]
                        last = mm(ps[:, 4 + 2 * (k % 2) + a // 4, (a % 4) * P:(a % 4 + 1) * P],
                                  s[:, hd, tile], rhs, start=True, stop=True)
                last.then_inc(prod, 1)

            for i in range(FB + 1):
                begin(i)
                for part in range(4):
                    last = project_part(i, part)
                last.then_inc(proj, 1)
            begin(IV)
            project_part(IV, 0)
            products(0)
            products(1)
            project_part(IV, 1).then_inc(proj, 1)
            products(2)
            products(3)
            begin(GZ)
            for part in range(4):
                last = project_part(GZ, part)
                if part < 3:
                    products(4 + part)
            last.then_inc(proj, 1)
            products(7)
            pe.wait_ge(conv_ok, TAPS * CH)
            pe.wait_ge(ev_act, 6)
            for c in range(CH):
                last = mm(ps[:, 3, 0:T], ones_c[:], acc[:, c, :], start=(c == 0), stop=(c == CH - 1))
            last.then_inc(mu_ps, 1)
            for k in range(8, 12):
                products(k)
            pe.wait_ge(xc2_ok, 1)
            for c in range(CH):
                last = mm(ps[:, 3, T:2 * T], ones_c[:], u[:, c, 0:T], start=(c == 0), stop=(c == CH - 1))
            last.then_inc(var_ps, 1)
            for k in range(12, N_STEP + 1):
                products(k)
            pe.wait_ge(lev, N_STEP + 1)
            pe.wait_ge(ev_dve, 3)
            for hd in range(H):
                vs = [v[:, t, hd * P:(hd + 1) * P] for t in range(NT)]
                for t in range(NT):
                    o = (hd % 2) * T + t * P
                    mm(ps[:, hd // 2, o:o + P], vs[t], am[:, hd, t, :], start=True, stop=False)
                    last = mm(ps[:, hd // 2, o:o + P], vs[1 - t], off[:, 1 - t, hd, :], start=False, stop=True)
            last.then_inc(av, 1)
            pe.wait_ge(o2_ok, 1)
            o2 = wk[:, 1].rearrange("p h t -> p (h t)")
            for i in range(2):
                last = mm(ps[:, 6 + i, :], ones_v[:], o2[:, i * 512:(i + 1) * 512], start=True, stop=True)
            last.then_inc(oms_ps, 1)

            def out_part(t, half, lo, hi):
                for c in range(lo, hi):
                    last = mm(ps[:, (4, 2)[half] + t, :], cat[:, c, t * P:(t + 1) * P],
                              ring[:, (N_IN + half) % SLOTS, c, :], start=(c == 4), stop=(c == 3))
                return last

            pe.wait_ge(catb_ok, 1)
            for half in range(2):
                pe.wait_ge(full[(N_IN + half) % SLOTS], 32)
                for t in range(NT):
                    out_part(t, half, 4, 8)
            pe.wait_ge(cata_ok, 1)
            for t in range(NT):
                for half in range(2):
                    last = out_part(t, half, 0, 4)
                    last.then_inc(oproj, 1)
            pe.wait_ge(oproj, 4)
            pe.wait_ge(n2_ok, NT)
            for c in range(C):
                bank = (0, 1, 6, 7)[c // 2]
                for t in range(NT):
                    last = tr(ps[:, bank, (c % 2) * T + t * P:(c % 2) * T + (t + 1) * P], n2[:, t, c * P:(c + 1) * P], ident)
                if c == 0:
                    last.then_inc(wout_done, 1)
                if c % 2:
                    last.then_inc(n2T_ps, 1)
            pe.wait_ge(n2T_sb, 2)
            pe.wait_ge(n2T_dve, 2)
            pe.wait_ge(r_in, 32)
            for t in range(NT):
                o = ps[:, 3, t * E:(t + 1) * E]
                for c in range(C):
                    mm(o, nT[:, c, t * P:(t + 1) * P], rw[:, c, :], start=(c == 0), stop=False)
                last = mm(o, ones[0:1, 0:P], rb[:], start=False, stop=True)
            last.then_inc(lgt_ps, 1)
            pe.wait_ge(sel_ok, 1)
            s = rt[:, 7]
            mm(ps[:, 3, 64:64 + E], tri, s[:, 0, :], start=True, stop=True)
            mm(ps[:, 3, 96:96 + E], tri, s[:, 1, :], start=True, stop=False)
            mm(ps[:, 3, 96:96 + E], ones[:, 0:P], s[:, 0, :], start=False, stop=True)
            mm(ps[:, 3, P:P + E], ones[:, 0:P], s[:, 0, :], start=True, stop=False)
            mm(ps[:, 3, P:P + E], ones[:, 0:P], s[:, 1, :], start=False, stop=True).then_inc(rank_ps, 1)
            pe.wait_ge(gates_ok, 1)
            for t in range(NT):
                last = tr(ps[0:E, 2, T + t * P:T + (t + 1) * P], gates[:, t, :], ident)
            last.then_inc(gT_ps, 1)
            pe.wait_ge(gT_sb, 1)
            pe.wait_ge(b2_in, 16)
            for t in range(NT):
                for half in range(2):
                    last = mm(ps[:, 4 + 2 * t + half, :], gT[:, t * P:(t + 1) * P],
                              b2_rows[:, half * CW:(half + 1) * CW], start=True, stop=True)
            last.then_inc(acc0, 1)

            def gather(n, part):
                pe.wait_ge(s_sel, n + 1)
                for c in range(4 * part, 4 * part + 4):
                    for t in range(NT):
                        last = mm(ps[:, 3, c * BLK:(c + 1) * BLK], n2[:, t, c * P:(c + 1) * P], sel[:, t, :],
                                  start=(t == 0), stop=(t == NT - 1))
                if part == 1:
                    last.then_inc(s_xps, 1)

            def multiply(n, uu):
                j, half = ORDER[uu]
                if half == 0:
                    if not (isinstance(n, int) and n == 0 and j < 2):
                        pe.wait_ge(s_ev, N_EXP * n + j - 1)
                    if j == 0:
                        pe.wait_ge(s_xl, n + 1)
                if j >= 4:
                    pe.wait_ge(s_al, 2 * n + half + 1)
                lhs = xg if j < 4 else aT
                for part, src, ready in ((0, wh, s_wh), (1, wl, s_wl)):
                    pe.wait_ge(ready, UNITS * n + uu + 1)
                    for c in range(4):
                        last = mm(ps[:, j % 2, :], lhs[:, 4 * half + c, :], src[:, uu % WD, c, :],
                                  start=(half == 0 and part == 0 and c == 0),
                                  stop=(half == 1 and part == 1 and c == 3))
                last.then_inc(s_mm, 1)

            def transpose_sum(n, j):
                pe.wait_ge(s_ev, N_EXP * n + j + 1)
                if j == 0 and not (isinstance(n, int) and n == 0):
                    pe.wait_ge(s_pre, 2 * n)
                if j == 2:
                    pe.wait_ge(s_pre, 2 * n + 1)
                for c in range(4):
                    o = (j % 2) * 4 * BLK + c * BLK
                    last = mm(ps[:, 2, o:o + BLK], hid[:, j % 2, c * P:(c + 1) * P], ident2, start=True, stop=True)
                last.then_inc(s_tr, 1)

            def gates_to_rows(n):
                pe.wait_ge(s_selg, n + 1)
                pe.wait_ge(s_xl, n + 1)
                for t in range(NT):
                    last = tr(ps[:, 3, t * P:(t + 1) * P], selg[:, t].rearrange("p a b -> p (a b)"), ident)
                last.then_inc(s_gps, 1)

            def combine(n, piece):
                if piece == 0:
                    pe.wait_ge(s_gt, n + 1)
                    pe.wait_ge(s_ev, N_EXP * n + 6)
                t, half = piece // 2, piece % 2
                mm(ps[:, 4 + piece, :], gsel[:, t, :], y[:, half * CW:(half + 1) * CW],
                   start=False, stop=True, skip_group_check=True).then_inc(s_comb, 1)

            def body(n, before, following):
                for uu in range(UNITS):
                    multiply(n, uu)
                    if uu == 1 and before:
                        gates_to_rows(n - 1)
                    if uu == 2:
                        transpose_sum(n, 0)
                    if uu == 4:
                        transpose_sum(n, 1)
                    if uu == 5:
                        if before:
                            combine(n - 1, 0)
                        if following:
                            gather(n + 1, 0)
                    if uu == 6:
                        transpose_sum(n, 2)
                        if following:
                            gather(n + 1, 1)
                    if uu == 7:
                        if before:
                            combine(n - 1, 1)
                        transpose_sum(n, 3)
                    if uu == 8 and before:
                        combine(n - 1, 2)
                        combine(n - 1, 3)

            def finish(n):
                gates_to_rows(n)
                for piece in range(NPC):
                    combine(n, piece)

            pe.wait_ge(routed, 1)
            gather(0, 0)
            gather(0, 1)
            body(0, False, True)
            with pe.Fori(1, E - 1) as n:
                body(n, True, True)
            body(E - 1, True, False)
            finish(E - 1)
            n_more = pe.value_load(nextra[0:1, 0:1], min_val=0, max_val=EXTRA)
            with pe.Fori(0, EXTRA) as i:
                with pe.If(i < n_more):
                    gather(E + i, 0)
                    gather(E + i, 1)
                    body(E + i, False, False)
                    finish(E + i)
                pe.nop()
            tr(ps[:, 2, 0:P], ident, ident).then_inc(y_all, 1)


def constants():
    import numpy as np
    c = np.zeros((P, K_END), np.float32)
    c[:, K_ID:K_ID + P] = np.eye(P)
    c[:, K_ID2:K_ID2 + BLK] = np.tile(np.eye(BLK), (2, 1))
    c[:, K_IOTA:K_IOTA + T] = np.arange(T)
    s, t = np.arange(P)[:, None], np.arange(P)[None, :]
    c[:, K_TRI:K_TRI + P] = s < t
    m = np.zeros((P, 2 * len(LEVELS) + 1, P), np.float32)
    for i, h in enumerate(LEVELS):
        m[:, i, :] = (s // (2 * h) == t // (2 * h)) & (s % (2 * h) < h) & (t % (2 * h) >= h)
        m[:, len(LEVELS) + i, :] = m[:, i, :].T
    m[:, 2 * len(LEVELS), :] = s == t
    return c, m


def kernel(x, norm1_w, w_in, lb_logits, hgrn_norm_w, dw_w, dw_b, conv_ln_w, conv_ln_b,
           w_out, norm2_w, router_w, router_b, w1, b1, w2, b2, final_norm_w):
    import numpy as np
    import concourse.bacc as bacc
    from concourse.bass_utils import run_bass_kernel_spmd
    c, m = constants()
    rows = lambda a: np.asarray(a).reshape(-1, P)
    ins = {
        "x": np.asarray(x)[0], "w_in": np.asarray(w_in)[0],
        "w_out": np.asarray(w_out)[0], "w1": np.asarray(w1)[0], "w2": np.asarray(w2)[0],
        "prm": np.concatenate([rows(lb_logits), rows(dw_b), rows(conv_ln_w), rows(conv_ln_b), rows(hgrn_norm_w),
                               rows(norm1_w)]),
        "dww": rows(dw_w), "b1": np.asarray(b1)[0], "b2": np.asarray(b2)[0],
        "router_w": np.asarray(router_w)[0], "router_b": np.asarray(router_b)[0],
        "norm2_w": np.asarray(norm2_w)[0], "final_w": np.asarray(final_norm_w), "consts": c, "masks": m,
    }
    ins = {k: np.ascontiguousarray(a) for k, a in ins.items()}
    nc = bacc.Bacc("TRN2", target_bir_lowering=False, num_devices=1)
    args = {k: nc.dram_tensor("in_" + k, a.shape, mybir.dt.from_np(a.dtype), kind="ExternalInput").ap()
            for k, a in ins.items()}
    out = nc.dram_tensor("out", (T, D), F32, kind="ExternalOutput").ap()
    encoder_layer(nc, out=out, **args)
    r = run_bass_kernel_spmd(nc, [{"in_" + k: a for k, a in ins.items()}], core_ids=[0])
    return r.results[0]["out"].reshape(1, T, D)
```

```python
import concourse.bass as bass
from concourse import mybir
from contextlib import ExitStack

F32 = mybir.dt.float32
F32R = mybir.dt.float32r
I32 = mybir.dt.int32
U8 = mybir.dt.uint8
ALU = mybir.AluOpType
ACT = mybir.ActivationFunctionType
AX = mybir.AxisListType

P = 128
T = 256
NT = T // P
D = 1024
C = D // P
H = 4
CH = 4
TAPS = 31
PAD = TAPS // 2
E = 32
TOPK = 4
CW = 512
SLOTS = 6
BLK = 64
EXTRA = (T * TOPK + E * (BLK - 1)) // BLK - E
LIMIT = 7.0
ALPHA = 1.702
EPS = 1e-5
HUGE = 3.0e38

CV, CG, FF, QZ, FB, IV, GZ = range(7)
W_IN_COLUMNS = [5, 6, 1, 0, 2, 3, 4]
N_IN = 7
N_FRONT = N_IN + 2
N_EXP = 6
LEVELS = [64, 32, 16, 8, 4, 2, 1]
UNITS = 2 * N_EXP
ORDER = [(j, a) for j in range(4) for a in (0, 1)] + [(4, 0), (5, 0), (4, 1), (5, 1)]
DONE = [max(i for i, u in enumerate(ORDER) if u[0] == j) + 1 for j in range(N_EXP)]
NPC = 4
PRM = 40
WD = 3

K_ID, K_ID2, K_IOTA, K_TRI = 0, 128, 192, 448
K_END = 576


def encoder_layer(nc, x, w_in, w_out, w1, w2, prm, dww, b1, b2, router_w, router_b,
                  norm2_w, final_w, consts, masks, out):
    w_in_v = w_in.rearrange("(c p) n -> p c n", p=P)
    w_out_v = w_out.rearrange("(c p) n -> p c n", p=P)
    w1_v = w1.rearrange("e (c p) n -> e p c n", p=P)
    w2_v = w2.rearrange("e (c p) n -> e p c n", p=P)
    x_v = x.rearrange("(i p) d -> p i d", p=P)
    out_v = out.rearrange("(i p) d -> p i d", p=P)

    keep = ExitStack()
    front = ExitStack()

    def sb(name, shape, dt=F32, stack=keep):
        return stack.enter_context(nc.sbuf_tensor(name, shape, dt))

    def sem(name):
        return keep.enter_context(nc.semaphore(name))

    with keep:
        ring = sb("ring", [P, SLOTS, C, CW])
        h = sb("h", [P, NT, D])
        n2 = sb("n2", [P, NT, D])
        cst = sb("cst", [P, K_END])
        wrow = sb("wrow", [P, D])
        b1T = sb("b1T", [P, 2 * C, E])
        gates = sb("gates", [P, NT, E])
        rankm = sb("rankm", [P, NT, E])
        table = sb("table", [1, 2, 16], I32)
        nextra = sb("nextra", [1, 1], I32)
        eps = sb("eps", [P, 1])
        ones = sb("ones", [P, T])
        ones_v = sb("ones_v", [P, P])
        ones_c = sb("ones_c", [P, P])
        ssum = sb("ssum", [P, 8])
        ident = cst[:, K_ID:K_ID + P]
        ident2 = cst[:, K_ID2:K_ID2 + BLK]
        iota = cst[:, K_IOTA:K_IOTA + T]
        tri = cst[:, K_TRI:K_TRI + P]

        nT = sb("nT", [P, C, T], stack=front)
        msk = sb("msk", [P, 2 * len(LEVELS) + 1, P], U8, front)
        q = sb("q", [P, H, T], stack=front)
        kf = sb("kf", [P, H, T], stack=front)
        kb = sb("kb", [P, H, T], stack=front)
        bf = sb("bf", [P, H, T], stack=front)
        bb = sb("bb", [P, H, T + 1], stack=front)
        v = sb("v", [P, NT, CW], stack=front)
        gate = sb("gate", [P, H, T], stack=front)
        cv = sb("cv", [P, CH, T], stack=front)
        u = sb("u", [P, CH, T + 2 * PAD], stack=front)
        acc = sb("acc", [P, CH, T], stack=front)
        ex = sb("ex", [P, 2, H, T], stack=front)
        wk = sb("wk", [P, 2, H, T], stack=front)
        am = sb("am", [P, H, NT, P], stack=front)
        off = sb("off", [P, 2, H, P], stack=front)
        cat = sb("cat", [P, C, T], stack=front)
        dwT = sb("dwT", [P, TAPS * CH], stack=front)
        prmT = sb("prmT", [P, PRM], stack=front)
        n1w = prmT[:, 32:32 + C]
        rw = sb("rw", [P, C, E], stack=front)
        rb = sb("rb", [1, E], stack=front)
        lbs = sb("lbs", [P, 6, 2, H], stack=front)
        orms = sb("orms", [P, 16], stack=front)
        lg = sb("lg", [P, NT, E], stack=front)
        mx = sb("mx", [P, NT, 8], stack=front)
        sm = sb("sm", [P, 8, NT], stack=front)
        flat = "p h t -> p (h t)"
        rt = bf[:].rearrange(flat)[:, 0:8 * NT * E].rearrange("p (k i e) -> p k i e", k=8, i=NT)
        msk_f = ex[:].rearrange("p a h t -> p (a h t)")[:, 0:(2 * len(LEVELS) + 1) * P]\
            .rearrange("p (m t) -> p m t", t=P)
        sA = cat[:, 0:4, :]
        sB = cat[:, 4:8, :]
        b1_rows = n2[0:E].rearrange("p a b -> p (a b)")
        tapped = gate
        rows = u[:, 0, 0:256].rearrange("p (a b) -> p a b", b=P)
        front.close()

        wh = sb("wh", [P, WD, 4, CW], F32R)
        wl = sb("wl", [P, WD, 4, CW], F32R)
        xg = sb("xg", [P, C, 2 * BLK], F32R)
        aT = sb("aT", [P, C, 2 * BLK], F32R)
        hid = sb("hid", [P, 2, CW])
        y = sb("y", [P, D])
        pre = sb("pre", [P, 2, 4, BLK])
        glu = sb("glu", [P, 4, BLK])
        lin = sb("lin", [P, 4, BLK])
        sig = sb("sig", [P, 4, BLK])
        gs = sb("gs", [P, 4, BLK])
        act_ = sb("act_", [P, 4, BLK])
        sel = sb("sel", [P, NT, BLK])
        selg = sb("selg", [P, NT, 2, BLK])
        gsel = sb("gsel", [P, NT, P])
        cur = sb("cur", [P, 4, NT])

        gT = sb("gT", [E, T])
        b2_rows = sb("b2_rows", [E, D])
        ctf = sb("ctf", [1, 3, E])
        cmp_ = sb("cmp_", [1, 2, EXTRA, E])
        eb = sb("eb", [1, 4, 16])

        ps = keep.enter_context(nc.psum_tensor("ps", [P, 8, 512], F32))

        def pair(i):
            return ps[:, 2 * i:2 * i + 2, :].rearrange("p a b -> p (a b)")

        def heads(ap):
            return ap.rearrange("p (h t) -> p h t", h=4)

        full = [sem(f"ring_full{s}") for s in range(SLOTS)]
        x_in, c_in, m_in, p_in, b1_in, b2_in, w2r_in, fw_in, r_in = [sem(n) for n in (
            "x_in", "consts_in", "masks_in", "params_in", "b1_in", "b2_in",
            "norm2_in", "final_in", "router_in")]
        (fills, sq1, rms1, xn_ok, xT_ok, nT_act, nT_dve, prm_ps, prm_sb, proj, ev_act, ev_dve,
         f_ok, logf_ok, sc_ok, e_ok, exp_ok, w_ok, prod, lev, ksum_ok, ksum_in) = [sem(n) for n in (
             "fills", "squares1", "rms1", "xn_ready", "xT_in_psum", "nT_by_act", "nT_by_dve",
             "params_in_psum", "params_ready", "projected", "evacuated_by_act", "evacuated_by_dve",
             "gate_ready", "log_gate_ready", "prefix_ready", "exponents_ready", "exps_ready",
             "scaled_ready", "level_products", "levels_merged", "key_sum_ready", "keys_ready")]
        (conv_ok, mu_ps, xc_ok, xc2_ok, var_ps, std_ok, ln_ok, lsg_ok, catb_ok) = [sem(n) for n in (
            "conv_ready", "conv_mean", "conv_centred", "conv_squares", "conv_var",
            "conv_std", "conv_normed", "conv_sigmoid", "cat_conv_ready")]
        (av, o2_ok, oms_ps, ostd_ok, cata_ok, oproj, h_ok, sq2, rms2, n2_ok, n2T_ps, n2T_sb,
         lgt_ps, lg_ok, ex4_ok, sel_ok, rank_ps, gates_ok, gT_ps, gT_sb, acc0, routed) = [sem(n) for n in (
             "attended", "o_squares", "o_mean_square", "o_rms", "cat_heads_ready",
             "out_projected", "h_ready", "squares2", "rms2", "n2_ready", "n2T_in_psum", "n2T_ready",
             "logits_in_psum", "logits_ready", "gate_exps", "chosen_ready", "ranks_in_psum",
             "gates_ready", "gatesT_in_psum", "gatesT_ready", "b2_summed", "routed")]
        (s_sel, s_selg, s_xps, s_xh, s_xl, s_wh, s_wl, s_mm, s_ev, s_tr, s_pre, s_glu, s_sig, s_gs,
         s_act, s_ah, s_al, s_gps, s_gt, s_comb, s_cur, s_lin) = [sem(n) for n in (
             "block_chosen", "block_gates", "gathered", "x_high", "x_low", "w_high", "w_low",
             "unit_multiplied", "chunk_evacuated", "hidden_transposed", "bias_added", "clamped",
             "sigmoid_ready", "gated_ready", "act_ready", "act_high", "act_low", "block_gatesT",
             "block_gatesT_ready", "combined", "columns_copied", "linear_clamped")]
        dve_seq, act_seq, pool_seq = sem("dve_seq"), sem("act_seq"), sem("pool_seq")
        y_all, y_sum, rms3, y_ok, y_out, n2T_dve, msk_ok, tabled, tap_ok, tap_sum, orec_ok, obc_ps, obc_ok = [sem(n) for n in (
            "experts_done", "y_sum", "rms3", "y_ready", "y_stored", "n2T_by_dve", "masks_ready", "extra_blocks_ready",
            "taps_multiplied", "taps_summed", "o_reciprocals", "o_scales_in_psum", "o_scales_ready")]

        def slot_of(j):
            return (N_FRONT + j) % SLOTS

        def filled(eng, n, j):
            eng.wait_ge(full[slot_of(j)], 16 * (n + (N_FRONT + j) // SLOTS + 1))

        def level_views(ap, hh):
            a = ap.rearrange("p h (n two j) -> p h n two j", two=2, j=hh)
            return a[:, :, :, 0, :], a[:, :, :, 1, :]

        steps = [(d, hh) for d in (0, 1) for hh in [P] + LEVELS]
        N_STEP = len(steps)
        block = keep.enter_context(nc.Block())

        @block.sync
        def _(sp):
            sp.dma_start(h[:], x_v).then_inc(x_in, 16)
            sp.dma_start(cst[:], consts).then_inc(c_in, 16)
            sp.dma_start(rows[0:TAPS * CH, 0, :], dww).then_inc(p_in, 16)
            sp.dma_start(rows[0:PRM, 1, :], prm).then_inc(p_in, 16)
            for i, col in enumerate(W_IN_COLUMNS):
                if i >= SLOTS:
                    sp.wait_ge(proj, i - SLOTS + 1)
                sp.dma_start(ring[:, i % SLOTS], w_in_v[:, :, col * CW:(col + 1) * CW])\
                  .then_inc(full[i % SLOTS], 16)
            for i in range(2):
                sp.wait_ge(proj, N_IN + i - SLOTS + 1)
                sp.dma_start(ring[:, (N_IN + i) % SLOTS], w_out_v[:, :, i * CW:(i + 1) * CW])\
                  .then_inc(full[(N_IN + i) % SLOTS], 16)

            def expert_chunk(e, j):
                if j < 4:
                    lo = (j // 2) * CW + (j % 2) * D
                    src = w1_v[e, :, :, lo:lo + CW]
                else:
                    src = w2_v[e, :, :, (j - 4) * CW:(j - 3) * CW]
                sp.dma_start(ring[:, slot_of(j)], src).then_inc(full[slot_of(j)], 16)

            def block_chunks(n, e):
                for j in range(N_EXP):
                    sp.wait_ge(s_wl, UNITS * (n - 1) + DONE[j])
                    expert_chunk(e, j)

            for j in range(N_EXP):
                if j < 4:
                    sp.wait_ge(proj, j + 4)
                else:
                    sp.wait_ge(oproj, 2 * NT)
                expert_chunk(0, j)
            with sp.Fori(1, E) as e:
                block_chunks(e, e)
            sp.wait_ge(tabled, 1)
            n_more = sp.value_load(nextra[0:1, 0:1], min_val=0, max_val=EXTRA)
            with sp.Fori(0, EXTRA) as i:
                with sp.If(i < n_more):
                    e = sp.value_load(table[0:1, 0, bass.ds(i, 1)], min_val=0, max_val=E - 1)
                    block_chunks(E + i, e)
                sp.nop()
            sp.wait_ge(y_ok, 1)
            sp.dma_start(out_v[:, 0, :], h[:, 0, :]).then_inc(y_out, 16)
            sp.wait_ge(y_ok, 2)
            sp.dma_start(out_v[:, 1, :], h[:, 1, :]).then_inc(y_out, 16)
            sp.wait_ge(y_out, 32)

        @block.gpsimd
        def _(pool):
            g = nc.gpsimd
            g.memset(eps[:], EPS).then_inc(fills, 1)
            g.memset(ones[:], 1.0).then_inc(fills, 1)
            g.memset(ones_v[:], 1.0 / P).then_inc(fills, 1)
            g.memset(ones_c[:], 1.0 / CW).then_inc(fills, 1)
            g.memset(bb[:, :, 0:1], 0.0).then_inc(fills, 1)
            g.memset(am[:], 0.0).then_inc(fills, 1)
            pool.wait_ge(prm_sb, 2)
            g.memset(u[:, :, 0:PAD], 0.0).then_inc(fills, 1)
            g.memset(u[:, :, PAD + T:], 0.0).then_inc(fills, 1)
            pool.wait_ge(m_in, 16)
            g.tensor_copy(msk[:], msk_f).then_inc(msk_ok, 1)
            for tap in range(1, TAPS):
                pool.wait_ge(tap_ok, tap + 1)
                if tap > 1:
                    pool.wait_ge(tap_sum, tap - 1)
                g.tensor_tensor(acc[:, 3, :], acc[:, 3, :], tapped[:, tap % 4, :], ALU.add).then_inc(tap_sum, 1)
            for k, (d, hh) in enumerate(steps):
                pool.wait_ge(exp_ok, k + 1)
                if k in (0, 8):
                    pool.wait_ge(f_ok, 2 + 2 * (k // 8))
                if k == 0:
                    pool.wait_ge(ev_dve, 2)
                if k >= 2:
                    pool.wait_ge(prod, k - 1)
                (ea, eb_), (wa, wb) = level_views(ex[:, k % 2], hh), level_views(wk[:, k % 2], hh)
                (qa, qb), (ka, kb_) = level_views(q[:], hh), level_views((kf, kb)[d][:], hh)
                first, second = (ka, qb) if d == 0 else (qa, kb_)
                g.tensor_tensor(wa, first, ea, ALU.mult)
                g.tensor_tensor(wb, second, eb_, ALU.mult).then_inc(w_ok, 1)
            pool.wait_ge(prod, N_STEP - 1)
            g.tensor_tensor(wk[:, 0], kf[:], kb[:], ALU.add).then_inc(w_ok, 1)

            def choose_gates(n, e):
                g.tensor_copy(cur[:, 1, :], gates[:, :, bass.ds(e, 1)].rearrange("p a b -> p (a b)"))\
                 .then_inc(s_cur, 1)
                if not (isinstance(n, int) and n == 0):
                    pool.wait_ge(s_gps, n)
                pool.wait_ge(s_cur, n + 1)
                pool.wait_ge(s_sel, n + 1)
                for t in range(NT):
                    last = g.tensor_tensor(selg[:, t], sel[:, t:t + 1, :].to_broadcast([P, 2, BLK]),
                                           cur[:, 1, t:t + 1].unsqueeze(2).to_broadcast([P, 2, BLK]), ALU.mult)
                last.then_inc(s_selg, 1)

            def gated(n, hf):
                pool.wait_ge(s_glu, 2 * n + hf + 1)
                pool.wait_ge(s_sig, 2 * n + hf + 1)
                g.tensor_tensor(gs[:], glu[:], sig[:], ALU.mult).then_inc(s_gs, 1)

            def body(n, e):
                choose_gates(n, e)
                gated(n, 0)
                gated(n, 1)

            pool.wait_ge(routed, 1)
            body(0, 0)
            with pool.Fori(1, E) as e:
                body(e, e)
            pool.wait_ge(tabled, 1)
            n_more = pool.value_load(nextra[0:1, 0:1], min_val=0, max_val=EXTRA)
            with pool.Fori(0, EXTRA) as i:
                with pool.If(i < n_more):
                    e = pool.value_load(table[0:1, 0, bass.ds(i, 1)], min_val=0, max_val=E - 1)
                    body(E + i, e)
                pool.nop()

        @block.scalar
        def _(act):
            a = nc.scalar
            act.dma_start(msk_f, masks).then_inc(m_in, 16)
            act.dma_start(wrow[:], norm2_w.partition_broadcast(P)).then_inc(w2r_in, 16)
            act.dma_start(rw[:], router_w.rearrange("(c p) e -> p c e", p=P)).then_inc(r_in, 16)
            act.dma_start(rb[:], router_b.rearrange("(a e) -> a e", a=1)).then_inc(r_in, 16)

            step = [0]

            def link(ins):
                step[0] += 1
                ins.then_inc(act_seq, 1)
                act.wait_ge(act_seq, step[0])

            act.wait_ge(fills, 1)
            act.wait_ge(x_in, 16)
            for t in range(NT):
                last = a.activation(wk[:, 0:2].rearrange("p a h t -> p a (h t)")[:, t], h[:, t, :], ACT.Square,
                                    accum_out=ssum[:, t:t + 1])
            link(last)
            a.activation(ssum[:, 2:4], ssum[:, 0:2], ACT.Sqrt, bias=eps[:], scale=1.0 / D).then_inc(rms1, 1)
            act.wait_ge(prm_sb, 2)
            for c in range(C // 2):
                act.wait_ge(xT_ok, c // 2 + 1)
                a.activation(nT[:, c, :], ps[:, 4 + c // 2, (c % 2) * T:(c % 2 + 1) * T], ACT.Copy, scale=n1w[:, c:c + 1])\
                 .then_inc(nT_act, 1)
            act.wait_ge(xT_ok, C // 2)
            act.dma_start(b1_rows, b1).then_inc(b1_in, 16)
            act.wait_ge(sc_ok, 1)
            a.activation(lbs[:, 2:4], lbs[:, 0:2], ACT.Exp).then_inc(sc_ok, 1)

            def exps(k):
                act.wait_ge(e_ok, k + 1)
                a.activation(ex[:, k % 2], ex[:, k % 2], ACT.Exp).then_inc(exp_ok, 1)

            def tap_products(lo, hi):
                for tap in range(lo, hi):
                    wt = dwT[:, tap * CH + 3:tap * CH + 4]
                    if tap == 0:
                        a.activation(acc[:, 3, :], u[:, 3, 0:T], ACT.Identity, scale=wt, bias=prmT[:, 19:20])\
                         .then_inc(tap_ok, 1)
                        continue
                    if tap > 4:
                        act.wait_ge(tap_sum, tap - 4)
                    a.activation(tapped[:, tap % 4, :], u[:, 3, tap:tap + T], ACT.Copy, scale=wt).then_inc(tap_ok, 1)

            act.wait_ge(proj, CV + 1)
            a.activation(cv[:], heads(pair(CV % 2)), ACT.Copy).then_inc(ev_act, 1)
            act.wait_ge(proj, CG + 1)
            a.activation(sA, heads(pair(CG % 2)), ACT.Sigmoid).then_inc(ev_act, 1)
            act.wait_ge(ev_dve, 1)
            tap_products(0, 16)
            act.wait_ge(proj, FF + 1)
            a.activation(sB, heads(pair(FF % 2)), ACT.Sigmoid).then_inc(ev_act, 1)
            act.wait_ge(f_ok, 2)
            a.activation(sB, sB, ACT.Ln).then_inc(logf_ok, 1)
            tap_products(16, TAPS)
            act.wait_ge(proj, QZ + 1)
            a.activation(sA, heads(pair(QZ % 2)), ACT.Sigmoid).then_inc(ev_act, 1)
            for k in range(0, 4):
                exps(k)
            act.wait_ge(proj, FB + 1)
            act.wait_ge(sc_ok, 3)
            a.activation(sB, heads(pair(FB % 2)), ACT.Sigmoid).then_inc(ev_act, 1)
            for k in range(4, 6):
                exps(k)
            act.wait_ge(f_ok, 4)
            a.activation(sB, sB, ACT.Ln).then_inc(logf_ok, 1)
            for k in range(6, 8):
                exps(k)
            act.wait_ge(proj, IV + 1)
            a.activation(v[:], pair(IV % 2).rearrange("p (t e) -> p t e", t=NT), ACT.Copy).then_inc(ev_act, 1)
            for k in range(8, 11):
                exps(k)
            act.wait_ge(xc_ok, 1)
            a.activation(u[:, :, 0:T], acc[:], ACT.Square).then_inc(xc2_ok, 1)
            for k in range(11, 13):
                exps(k)
            act.wait_ge(var_ps, 1)
            a.activation(u[:, 0, 0:T], ps[:, 3, T:2 * T], ACT.Sqrt, bias=eps[:]).then_inc(std_ok, 1)
            for k in range(13, N_STEP):
                exps(k)
            act.wait_ge(proj, GZ + 1)
            a.activation(sA, heads(pair(GZ % 2)), ACT.Sigmoid).then_inc(ev_act, 1)
            act.wait_ge(ln_ok, 1)
            for c in range(CH):
                last = a.activation(u[:, c, 0:T], acc[:, c, :], ACT.Sigmoid,
                                    scale=prmT[:, 20 + c:21 + c], bias=prmT[:, 24 + c:25 + c])
            last.then_inc(lsg_ok, 1)
            act.wait_ge(av, 1)
            a.activation(wk[:, 1], heads(pair(0)), ACT.Square).then_inc(o2_ok, 1)
            act.wait_ge(oms_ps, 1)
            a.activation(orms[:, 0:8], ps[:, 6, 0:8], ACT.Sqrt, bias=eps[:]).then_inc(ostd_ok, 1)
            act.wait_ge(obc_ps, 1)
            a.activation(ex[:, 0], heads(pair(3)), ACT.Copy).then_inc(obc_ok, 1)
            for t in range(NT):
                act.wait_ge(h_ok, t + 1)
                link(a.activation(ex[:, 0:2].rearrange("p a h t -> p a (h t)")[:, t], h[:, t, :], ACT.Square,
                                  accum_out=ssum[:, t:t + 1]))
                a.activation(ssum[:, 2 + t:3 + t], ssum[:, t:t + 1], ACT.Sqrt, bias=eps[:], scale=1.0 / D)\
                 .then_inc(rms2, 1)
            act.wait_ge(oproj, 4)
            act.dma_start(b2_rows[:], b2).then_inc(b2_in, 16)
            act.wait_ge(n2_ok, NT)
            act.dma_start(wrow[:], final_w.partition_broadcast(P)).then_inc(fw_in, 16)
            for t in range(NT):
                act.wait_ge(n2T_ps, t + 1)
                a.activation(nT[:, 0:4, t * P:(t + 1) * P], ps[:, 6 * t, :].rearrange("p (c t) -> p c t", c=4), ACT.Copy)\
                 .then_inc(n2T_sb, 1)
            act.wait_ge(lg_ok, 1)
            act.wait_ge(lgt_ps, 1)
            for t in range(NT):
                last = a.activation(rt[:, 0, t, :], lg[:, t, :], ACT.Exp, bias=sm[:, 0, t:t + 1])
            last.then_inc(ex4_ok, 1)
            def split_high(n, uu):
                j, half = ORDER[uu]
                if half == 0:
                    filled(act, n, j)
                if not (isinstance(n, int) and UNITS * n + uu < WD):
                    act.wait_ge(s_mm, UNITS * n + uu + 1 - WD)
                a.activation(wh[:, uu % WD], ring[:, slot_of(j), 4 * half:4 * half + 4, :], ACT.Copy)\
                 .then_inc(s_wh, 1)

            def evacuate(n, j):
                act.wait_ge(s_mm, UNITS * n + DONE[j])
                if j < 4:
                    if j >= 2:
                        act.wait_ge(s_tr, 4 * n + j - 1)
                    dst = hid[:, j % 2, :]
                else:
                    dst = y[:, (j - 4) * CW:(j - 3) * CW]
                a.activation(dst, ps[:, j % 2, :], ACT.Copy).then_inc(s_ev, 1)

            def x_high(n):
                act.wait_ge(s_xps, n + 1)
                if not (isinstance(n, int) and n == 0):
                    act.wait_ge(s_mm, UNITS * (n - 1) + DONE[3])
                a.activation(xg[:, :, 0:BLK], ps[:, 3, :].rearrange("p (c s) -> p c s", c=C), ACT.Copy)\
                 .then_inc(s_xh, 1)

            def gates_out(n):
                act.wait_ge(s_gps, n + 1)
                a.activation(gsel[:], ps[:, 3, 0:T].rearrange("p (i t) -> p i t", i=NT), ACT.Copy).then_inc(s_gt, 1)

            def sigmoid(n, hf):
                act.wait_ge(s_glu, 2 * n + hf + 1)
                a.activation(sig[:], glu[:], ACT.Sigmoid, scale=ALPHA).then_inc(s_sig, 1)

            def a_high(n, hf):
                act.wait_ge(s_act, 2 * n + hf + 1)
                a.activation(aT[:, 4 * hf:4 * hf + 4, 0:BLK], act_[:], ACT.Copy).then_inc(s_ah, 1)

            def y_out_of(n, j):
                if not (isinstance(n, int) and n == 0) and j == 4:
                    act.wait_ge(s_comb, NPC * n)
                evacuate(n, j)

            def body(n, before, following, first=0):
                for uu in range(first, UNITS):
                    split_high(n, uu)
                    if uu < 2 and before:
                        y_out_of(n - 1, 4 + uu)
                    if uu == 3:
                        evacuate(n, 0)
                    if uu == 4 and before:
                        gates_out(n - 1)
                    if uu == 5:
                        evacuate(n, 1)
                    if uu == 7:
                        evacuate(n, 2)
                    if uu == 8:
                        sigmoid(n, 0)
                    if uu == 9:
                        a_high(n, 0)
                        evacuate(n, 3)
                    if uu == 10:
                        sigmoid(n, 1)
                        if following:
                            x_high(n + 1)
                        a_high(n, 1)

            def finish(n):
                y_out_of(n, 4)
                y_out_of(n, 5)
                gates_out(n)

            split_high(0, 0)
            act.wait_ge(gT_ps, 1)
            a.activation(gT[:], ps[0:E, 2, T:2 * T], ACT.Copy).then_inc(gT_sb, 1)
            split_high(0, 1)
            x_high(0)
            act.wait_ge(routed, 1)
            body(0, False, True, 2)
            with act.Fori(1, E - 1) as n:
                body(n, True, True)
            body(E - 1, True, False)
            finish(E - 1)
            act.wait_ge(tabled, 1)
            n_more = act.value_load(nextra[0:1, 0:1], min_val=0, max_val=EXTRA)
            with act.Fori(0, EXTRA) as i:
                with act.If(i < n_more):
                    x_high(E + i)
                    body(E + i, False, False)
                    finish(E + i)
                act.nop()
            for t in range(NT):
                act.wait_ge(y_sum, t + 1)
                last = a.activation(n2[:, t, :], h[:, t, :], ACT.Square, accum_out=ssum[:, t:t + 1])
            link(last)
            a.activation(ssum[:, 2:4], ssum[:, 0:2], ACT.Sqrt, bias=eps[:], scale=1.0 / D).then_inc(rms3, 1)

        @block.vector
        def _(dve):
            w = nc.vector
            step = [0]

            def link(ins):
                step[0] += 1
                ins.then_inc(dve_seq, 1)
                dve.wait_ge(dve_seq, step[0])

            dve.wait_ge(rms1, 1)
            link(w.reciprocal(ssum[:, 4:6], ssum[:, 2:4]))
            for t in range(NT):
                w.tensor_scalar(n2[:, t, :], h[:, t, :], ssum[:, 4 + t:5 + t], None, ALU.mult).then_inc(xn_ok, 1)
            dve.wait_ge(prm_ps, 1)
            w.tensor_copy(dwT[:], ps[:, 0, 0:TAPS * CH])
            w.tensor_copy(prmT[:], ps[:, 0, P:P + PRM]).then_inc(prm_sb, 2)
            dve.wait_ge(prm_sb, 2)
            for c in range(C // 2, C):
                dve.wait_ge(xT_ok, c // 2 + 1)
                w.tensor_scalar(nT[:, c, :], ps[:, 4 + c // 2, (c % 2) * T:(c % 2 + 1) * T], n1w[:, c:c + 1], None, ALU.mult)\
                 .then_inc(nT_dve, 1)
            lbv = prmT[:, 0:16].rearrange("p (d r h) -> p r d h", d=2, r=2)
            link(w.tensor_tensor(lbs[:, 4], lbv[:, 0], lbv[:, 1], ALU.max))
            w.tensor_tensor(lbs[:, 0], lbv[:, 0], lbs[:, 4], ALU.subtract)
            w.tensor_tensor(lbs[:, 1], lbv[:, 1], lbs[:, 4], ALU.subtract).then_inc(sc_ok, 1)
            dve.wait_ge(sc_ok, 2)
            link(w.tensor_tensor(lbs[:, 4], lbs[:, 2], lbs[:, 3], ALU.add))
            link(w.reciprocal(lbs[:, 5], lbs[:, 4]))
            link(w.tensor_tensor(lbs[:, 0], lbs[:, 2], lbs[:, 5], ALU.mult))
            link(w.tensor_scalar(lbs[:, 1], lbs[:, 0], -1.0, 1.0, ALU.mult, ALU.add))

            def conv(lo, hi):
                for tap in range(lo, hi):
                    for c in range(CH - 1):
                        wt = dwT[:, tap * CH + c:tap * CH + c + 1]
                        if tap == 0:
                            ins = w.tensor_scalar(acc[:, c, :], u[:, c, 0:T], wt, prmT[:, 16 + c:17 + c],
                                                  ALU.mult, ALU.add)
                        else:
                            dve.wait_ge(conv_ok, (tap - 1) * (CH - 1) + c + 1)
                            ins = w.scalar_tensor_tensor(out=acc[:, c, :], in0=u[:, c, tap:tap + T], scalar=wt,
                                                         in1=acc[:, c, :], op0=ALU.mult, op1=ALU.add)
                        ins.then_inc(conv_ok, 1)

            def gates_of(d):
                dve.wait_ge(ev_act, (FF, FB)[d] + 1)
                for hd in range(H):
                    last = w.tensor_scalar(sB[:, hd, :], sB[:, hd, :], lbs[:, 1, d, hd:hd + 1],
                                           lbs[:, 0, d, hd:hd + 1], ALU.mult, ALU.add)
                last.then_inc(f_ok, 1)
                dve.wait_ge(f_ok, 2 * d + 1)
                w.tensor_scalar((kf, kb)[d][:], sB, -1.0, 1.0, ALU.mult, ALU.add).then_inc(f_ok, 1)

            def prefix(d):
                dve.wait_ge(logf_ok, d + 1)
                for hd in range(H):
                    dst = bf[:, hd, :] if d == 0 else bb[:, hd, 1:T + 1]
                    last = w.tensor_tensor_scan(dst, ones[:], sB[:, hd, :], 0.0, ALU.mult, ALU.add)
                last.then_inc(sc_ok, 1)
                dve.wait_ge(sc_ok, 3 + d)

            def exponents(k):
                d, hh = steps[k]
                b = bf[:] if d == 0 else bb[:, :, 0:T]
                if k >= 2:
                    dve.wait_ge(w_ok, k - 1)
                first, second = level_views(b, hh)
                ea, eb_ = level_views(ex[:, k % 2], hh)
                mid = first[:, :, :, hh - 1:hh] if d == 0 else second[:, :, :, 0:1]
                mid = mid.to_broadcast([P, H, T // (2 * hh), hh])
                w.tensor_tensor(ea, mid, first, ALU.subtract)
                w.tensor_tensor(eb_, second, mid, ALU.subtract).then_inc(e_ok, 1)

            def merge(k):
                dve.wait_ge(prod, k + 1)
                if k < N_STEP and steps[k][1] == P:
                    w.tensor_copy(off[:, steps[k][0]], ps[:, 4 + 2 * (k % 2), :].rearrange("p (h t) -> p h t", h=H))\
                     .then_inc(lev, 1)
                    return
                if k < N_STEP:
                    m = len(LEVELS) * steps[k][0] + LEVELS.index(steps[k][1])
                else:
                    m = 2 * len(LEVELS)
                dve.wait_ge(lev, k)
                mk = msk[:, m:m + 1, :].to_broadcast([P, H * NT, P])
                w.copy_predicated(am[:].rearrange("p h i t -> p (h i) t"), mk,
                                  pair(2 + k % 2).rearrange("p (a t) -> p a t", t=P)).then_inc(lev, 1)

            dve.wait_ge(fills, 8)
            dve.wait_ge(ev_act, CG + 1)
            w.tensor_tensor(u[:, :, PAD:PAD + T], cv[:], sA, ALU.mult).then_inc(ev_dve, 1)
            dve.wait_ge(ev_dve, 1)
            conv(0, 11)
            gates_of(0)
            conv(11, 13)
            prefix(0)
            dve.wait_ge(msk_ok, 1)
            exponents(0)
            exponents(1)
            dve.wait_ge(prm_ps, 2)
            w.tensor_copy(b1T[:], ps[:, 4, :].rearrange("p (c e) -> p c e", e=E)).then_inc(prm_sb, 1)
            conv(13, 15)
            dve.wait_ge(ev_act, QZ + 1)
            w.tensor_tensor(q[:], heads(pair(QZ % 2)), sA, ALU.mult).then_inc(ev_dve, 1)
            for k in range(0, N_STEP):
                if k == 4:
                    gates_of(1)
                if k == 6:
                    prefix(1)
                if k + 2 < N_STEP:
                    exponents(k + 2)
                if k < 8:
                    conv(15 + 2 * k, 17 + 2 * k)
                if k == 9:
                    dve.wait_ge(mu_ps, 1)
                    w.tensor_tensor(acc[:], acc[:], ps[:, 3:4, 0:T].to_broadcast([P, CH, T]), ALU.subtract)\
                     .then_inc(xc_ok, 1)
                if k == 13:
                    dve.wait_ge(std_ok, 1)
                    link(w.reciprocal(u[:, 1, 0:T], u[:, 0, 0:T]))
                    w.tensor_tensor(acc[:], acc[:], u[:, 1:2, 0:T].to_broadcast([P, CH, T]), ALU.mult)\
                     .then_inc(ln_ok, 1)
                merge(k)
            dve.wait_ge(ev_act, GZ + 1)
            w.tensor_tensor(gate[:], heads(pair(GZ % 2)), sA, ALU.mult).then_inc(ev_dve, 1)
            merge(N_STEP)
            dve.wait_ge(lsg_ok, 1)
            for c in range(CH):
                last = w.tensor_scalar(acc[:, c, :], acc[:, c, :], prmT[:, 20 + c:21 + c], prmT[:, 24 + c:25 + c],
                                       ALU.mult, ALU.add)
            link(last)
            w.tensor_tensor(cat[:, 4:8, :], acc[:], u[:, :, 0:T], ALU.mult).then_inc(catb_ok, 1)
            dve.wait_ge(ostd_ok, 1)
            w.reciprocal(orms[:, 8:16], orms[:, 0:8]).then_inc(orec_ok, 1)
            dve.wait_ge(obc_ok, 1)
            link(w.tensor_tensor(wk[:, 0], heads(pair(0)), ex[:, 0], ALU.mult))
            for hd in range(H):
                last = w.scalar_tensor_tensor(out=cat[:, hd, :], in0=wk[:, 0, hd, :], scalar=prmT[:, 28 + hd:29 + hd],
                                              in1=gate[:, hd, :], op0=ALU.mult, op1=ALU.mult)
            last.then_inc(cata_ok, 1)
            dve.wait_ge(w2r_in, 16)
            for t in range(NT):
                for half in range(2):
                    dve.wait_ge(oproj, 2 * t + half + 1)
                    cols = slice(half * CW, (half + 1) * CW)
                    last = w.tensor_tensor(h[:, t, cols], h[:, t, cols], ps[:, (4, 2)[half] + t, :], ALU.add)
                last.then_inc(h_ok, 1)
                dve.wait_ge(rms2, t + 1)
                link(w.reciprocal(ssum[:, 4 + t:5 + t], ssum[:, 2 + t:3 + t]))
                w.scalar_tensor_tensor(out=n2[:, t, :], in0=h[:, t, :], scalar=ssum[:, 4 + t:5 + t], in1=wrow[:],
                                       op0=ALU.mult, op1=ALU.mult).then_inc(n2_ok, 1)
            for t in range(NT):
                dve.wait_ge(n2T_ps, t + 1)
                w.tensor_copy(nT[:, 4:8, t * P:(t + 1) * P], ps[:, 6 * t + 1, :].rearrange("p (c t) -> p c t", c=4))\
                 .then_inc(n2T_dve, 1)
            dve.wait_ge(lgt_ps, 1)
            link(w.tensor_copy(lg[:], ps[:, 3, 0:NT * E].rearrange("p (i e) -> p i e", i=NT)))
            for t in range(NT):
                last = w.max(mx[:, t, :], lg[:, t, :])
            link(last)
            w.tensor_scalar(sm[:, 0, :], mx[:, :, 0], -1.0, None, ALU.mult).then_inc(lg_ok, 1)
            v4 = mx[:, :, TOPK - 1:TOPK].to_broadcast([P, NT, E])
            w.tensor_tensor(rt[:, 1], lg[:], v4, ALU.is_gt)
            link(w.tensor_tensor(rt[:, 2], lg[:], v4, ALU.is_equal))
            w.tensor_reduce(sm[:, 1, :], rt[:, 1], AX.X, ALU.add)
            for t in range(NT):
                last = w.tensor_tensor_scan(rt[:, 3, t, :], ones[:, 0:E], rt[:, 2, t, :], 0.0, ALU.mult, ALU.add)
            link(last)
            link(w.tensor_tensor(rt[:, 4], rt[:, 3], sm[:, 1, :].unsqueeze(2).to_broadcast([P, NT, E]), ALU.add))
            link(w.tensor_scalar(rt[:, 5], rt[:, 4], float(TOPK), None, ALU.is_le))
            link(w.tensor_tensor(rt[:, 6], rt[:, 5], rt[:, 2], ALU.mult))
            w.tensor_tensor(rt[:, 7], rt[:, 6], rt[:, 1], ALU.add).then_inc(sel_ok, 1)
            dve.wait_ge(sel_ok, 1)
            dve.wait_ge(ex4_ok, 1)
            link(w.tensor_tensor(rt[:, 1], rt[:, 0], rt[:, 7], ALU.mult))
            link(w.tensor_reduce(sm[:, 2, :], rt[:, 1], AX.X, ALU.add))
            link(w.reciprocal(sm[:, 3, :], sm[:, 2, :]))
            w.tensor_tensor(gates[:], rt[:, 1], sm[:, 3, :].unsqueeze(2).to_broadcast([P, NT, E]), ALU.mult)\
             .then_inc(gates_ok, 1)
            dve.wait_ge(rank_ps, 1)
            link(w.scalar_tensor_tensor(out=rt[:, 2], in0=ps[:, 3, 64:64 + NT * E].rearrange("p (i e) -> p i e", i=NT),
                                        scalar=1.0, in1=rt[:, 7], op0=ALU.add, op1=ALU.mult))
            w.tensor_scalar(rankm[:], rt[:, 2], 1.0, None, ALU.subtract)
            w.tensor_copy(ctf[0:1, 0, :], ps[0:1, 3, P:P + E]).then_inc(routed, 1)

            def extra_blocks():
                link(w.tensor_scalar(ctf[0:1, 1, :], ctf[0:1, 0, :], float(BLK), None, ALU.is_gt))
                for k in range(2, T // BLK):
                    link(w.scalar_tensor_tensor(out=ctf[0:1, 1, :], in0=ctf[0:1, 0, :], scalar=float(k * BLK),
                                                in1=ctf[0:1, 1, :], op0=ALU.is_gt, op1=ALU.add))
                link(w.tensor_tensor_scan(ctf[0:1, 2, :], ones[0:1, 0:E], ctf[0:1, 1, :], 0.0, ALU.mult, ALU.add))
                jj = iota[0:1, 0:EXTRA].unsqueeze(2).to_broadcast([1, EXTRA, E])
                link(w.tensor_tensor(cmp_[0:1, 0], ctf[0:1, 2:3, :].to_broadcast([1, EXTRA, E]), jj, ALU.is_le))
                link(w.tensor_tensor(cmp_[0:1, 1], ctf[0:1, 1:2, :].to_broadcast([1, EXTRA, E]), cmp_[0:1, 0], ALU.mult))
                w.tensor_reduce(eb[0:1, 0, 0:EXTRA], cmp_[0:1, 0], AX.X, ALU.add)
                link(w.tensor_reduce(eb[0:1, 1, 0:EXTRA], cmp_[0:1, 1], AX.X, ALU.add))
                link(w.tensor_tensor(eb[0:1, 2, 0:EXTRA], iota[0:1, 0:EXTRA], eb[0:1, 1, 0:EXTRA], ALU.subtract))
                link(w.tensor_scalar(eb[0:1, 3, 0:EXTRA], eb[0:1, 2, 0:EXTRA], float(BLK), float(BLK), ALU.mult, ALU.add))
                w.tensor_scalar(table[0:1, 0, 0:EXTRA], eb[0:1, 0, 0:EXTRA], float(E - 1), None, ALU.min)
                w.tensor_scalar(table[0:1, 1, 0:EXTRA], eb[0:1, 3, 0:EXTRA], float(T - BLK), None, ALU.min)
                w.tensor_copy(nextra[:], ctf[0:1, 2, E - 1:E]).then_inc(tabled, 1)

            def split_low(n, uu):
                dve.wait_ge(s_wh, UNITS * n + uu + 1)
                if not (isinstance(n, int) and UNITS * n + uu < WD):
                    dve.wait_ge(s_mm, UNITS * n + uu + 1 - WD)
                j, half = ORDER[uu]
                w.tensor_tensor(wl[:, uu % WD], ring[:, slot_of(j), 4 * half:4 * half + 4, :],
                                wh[:, uu % WD].bitcast(F32), ALU.subtract).then_inc(s_wl, 1)

            def x_low(n):
                dve.wait_ge(s_xh, n + 1)
                w.tensor_tensor(xg[:, :, BLK:2 * BLK], ps[:, 3, :].rearrange("p (c s) -> p c s", c=C),
                                xg[:, :, 0:BLK].bitcast(F32), ALU.subtract).then_inc(s_xl, 1)

            def choose(n, e, r):
                if not (isinstance(n, int) and n == 0):
                    dve.wait_ge(s_xps, n)
                    dve.wait_ge(s_selg, n)
                for t in range(NT):
                    last = w.tensor_scalar(sel[:, t, :], iota[:, bass.ds(r, BLK)],
                                           rankm[:, t, bass.ds(e, 1)], None, ALU.is_equal)
                last.then_inc(s_sel, 1)

            def add_bias(n, e, hf):
                dve.wait_ge(s_tr, 4 * n + 2 * hf + 2)
                if not (isinstance(n, int) and n == 0 and hf == 0):
                    dve.wait_ge(s_lin, 2 * n + hf)
                bias = b1T[:, :, bass.ds(e, 1)].rearrange("p (g c) o -> p g c o", g=2)[:, :, 4 * hf:4 * hf + 4, :]
                w.tensor_tensor(pre[:], ps[:, 2, :].rearrange("p (g c s) -> p g c s", g=2, c=4),
                                bias.to_broadcast([P, 2, 4, BLK]), ALU.add).then_inc(s_pre, 1)
                dve.wait_ge(s_pre, 2 * n + hf + 1)
                if not (isinstance(n, int) and n == 0 and hf == 0):
                    dve.wait_ge(s_gs, 2 * n + hf)
                w.tensor_scalar(glu[:], pre[:, 0], LIMIT, None, ALU.min).then_inc(s_glu, 1)
                w.tensor_scalar(lin[:], pre[:, 1], LIMIT, -LIMIT, ALU.min, ALU.max).then_inc(s_lin, 1)

            def activate(n, hf):
                dve.wait_ge(s_gs, 2 * n + hf + 1)
                dve.wait_ge(s_lin, 2 * n + hf + 1)
                if not (isinstance(n, int) and n == 0 and hf == 0):
                    dve.wait_ge(s_al, 2 * n + hf)
                w.scalar_tensor_tensor(out=act_[:], in0=lin[:], scalar=1.0, in1=gs[:], op0=ALU.add, op1=ALU.mult)\
                 .then_inc(s_act, 1)

            def a_low(n, hf):
                dve.wait_ge(s_ah, 2 * n + hf + 1)
                w.tensor_tensor(aT[:, 4 * hf:4 * hf + 4, BLK:2 * BLK], act_[:],
                                aT[:, 4 * hf:4 * hf + 4, 0:BLK].bitcast(F32), ALU.subtract).then_inc(s_al, 1)

            def body(n, e, following, first=0):
                for uu in range(first, UNITS):
                    split_low(n, uu)
                    if uu == 4 and following:
                        choose(n + 1, e + 1, 0)
                    if uu == 6:
                        add_bias(n, e, 0)
                    if uu == 8:
                        activate(n, 0)
                    if uu == 9:
                        a_low(n, 0)
                        add_bias(n, e, 1)
                    if uu == 10:
                        activate(n, 1)
                        a_low(n, 1)
                    if uu == 11 and following:
                        x_low(n + 1)

            dve.wait_ge(routed, 1)
            choose(0, 0, 0)
            split_low(0, 0)
            split_low(0, 1)
            x_low(0)
            body(0, 0, True, 2)
            extra_blocks()
            with dve.Fori(1, E - 1) as n:
                body(n, n, True)
            body(E - 1, E - 1, False)
            dve.wait_ge(tabled, 1)
            n_more = dve.value_load(nextra[0:1, 0:1], min_val=0, max_val=EXTRA)
            with dve.Fori(0, EXTRA) as i:
                with dve.If(i < n_more):
                    e = dve.value_load(table[0:1, 0, bass.ds(i, 1)], min_val=0, max_val=E - 1)
                    r = dve.value_load(table[0:1, 1, bass.ds(i, 1)], min_val=0, max_val=T - BLK)
                    choose(E + i, e, r)
                    x_low(E + i)
                    body(E + i, e, False)
                dve.nop()
            dve.wait_ge(y_all, 1)
            for t in range(NT):
                w.tensor_tensor(h[:, t, :], h[:, t, :], ps[:, 4 + 2 * t:6 + 2 * t, :].rearrange("p a b -> p (a b)"),
                                ALU.add).then_inc(y_sum, 1)
            dve.wait_ge(rms3, 1)
            dve.wait_ge(fw_in, 16)
            link(w.reciprocal(ssum[:, 4:6], ssum[:, 2:4]))
            for t in range(NT):
                w.scalar_tensor_tensor(out=h[:, t, :], in0=h[:, t, :], scalar=ssum[:, 4 + t:5 + t], in1=wrow[:],
                                       op0=ALU.mult, op1=ALU.mult).then_inc(y_ok, 1)

        @block.tensor
        def _(pe):
            mm, tr = nc.tensor.matmul, nc.tensor.transpose
            pe.wait_ge(c_in, 16)
            pe.wait_ge(p_in, 32)
            tr(ps[:, 0, 0:TAPS * CH], rows[0:TAPS * CH, 0, :], ident[0:TAPS * CH, 0:TAPS * CH])
            tr(ps[:, 0, P:P + PRM], rows[0:PRM, 1, :], ident[0:PRM, 0:PRM]).then_inc(prm_ps, 1)
            pe.wait_ge(xn_ok, NT)
            for c in range(C):
                for t in range(NT):
                    last = tr(ps[:, 4 + c // 2, (c % 2) * T + t * P:(c % 2) * T + (t + 1) * P],
                              n2[:, t, c * P:(c + 1) * P], ident)
                if c % 2:
                    last.then_inc(xT_ok, 1)
            pe.wait_ge(nT_act, C // 2)
            pe.wait_ge(nT_dve, C // 2)

            def project_part(i, part):
                wt = ring[:, i % SLOTS]
                base = 2 * (i % 2)
                for c in range(C):
                    if i == IV:
                        last = mm(ps[:, base + part, :], nT[:, c, part * P:(part + 1) * P], wt[:, c, :],
                                  start=(c == 0), stop=(c == C - 1))
                    else:
                        o = (part % 2) * T
                        last = mm(ps[:, base + part // 2, o:o + T], wt[:, c, part * P:(part + 1) * P],
                                  nT[:, c, :], start=(c == 0), stop=(c == C - 1))
                return last

            def begin(i):
                pe.wait_ge(full[i % SLOTS], 16 * (i // SLOTS + 1))
                if i >= 2:
                    pe.wait_ge(ev_act, i - 1)
                    if i - 2 == QZ:
                        pe.wait_ge(ev_dve, 2)

            def products(k):
                pe.wait_ge(w_ok, k + 1)
                if k >= 2:
                    pe.wait_ge(lev, k - 1)
                s = wk[:, k % 2]
                for hd in range(H):
                    if k < N_STEP and steps[k][1] == P:
                        d = steps[k][0]
                        last = mm(ps[:, 4 + 2 * (k % 2), hd * P:(hd + 1) * P], s[:, hd, d * P:(d + 1) * P],
                                  s[:, hd, (1 - d) * P:(2 - d) * P], start=True, stop=True)
                        continue
                    for t in range(NT):
                        a = hd * NT + t
                        tile = slice(t * P, (t + 1) * P)
                        rhs = s[:, hd, tile] if k < N_STEP else q[:, hd, tile]
                        last = mm(ps[:, 4 + 2 * (k % 2) + a // 4, (a % 4) * P:(a % 4 + 1) * P],
                                  s[:, hd, tile], rhs, start=True, stop=True)
                last.then_inc(prod, 1)

            def mean():
                pe.wait_ge(conv_ok, TAPS * (CH - 1))
                pe.wait_ge(tap_sum, TAPS - 1)
                pe.wait_ge(ev_act, IV + 1)
                for c in range(CH):
                    last = mm(ps[:, 3, 0:T], ones_c[:], acc[:, c, :], start=(c == 0), stop=(c == CH - 1))
                last.then_inc(mu_ps, 1)

            def variance():
                pe.wait_ge(xc2_ok, 1)
                for c in range(CH):
                    last = mm(ps[:, 3, T:2 * T], ones_c[:], u[:, c, 0:T], start=(c == 0), stop=(c == CH - 1))
                last.then_inc(var_ps, 1)

            def project(i, then={}):
                begin(i)
                parts = NT if i == IV else 4
                for part in range(parts):
                    last = project_part(i, part)
                    if part == parts - 1:
                        last.then_inc(proj, 1)
                    for other in then.get(part, ()):
                        if isinstance(other, int):
                            products(other)
                        else:
                            other()

            def b1_to_columns():
                pe.wait_ge(b1_in, 16)
                for c in range(2 * C):
                    last = tr(ps[:, 4, c * E:(c + 1) * E], b1_rows[:, c * P:(c + 1) * P], ident[0:E, 0:E])
                last.then_inc(prm_ps, 1)

            project(CV)
            project(CG)
            project(FF)
            b1_to_columns()
            project(QZ)
            pe.wait_ge(prm_sb, 3)
            project(FB, {1: [0], 2: [1], 3: [2]})
            project(IV, {0: [3, 4], 1: [5, 6]})
            project(GZ, {0: [7, mean, 8], 1: [9, 10], 2: [variance, 11, 12], 3: [13]})
            for k in range(14, N_STEP + 1):
                products(k)
            pe.wait_ge(lev, N_STEP + 1)
            pe.wait_ge(ev_dve, 3)
            pe.wait_ge(lev, N_STEP + 1)
            pe.wait_ge(ev_dve, 3)
            for hd in range(H):
                vs = [v[:, t, hd * P:(hd + 1) * P] for t in range(NT)]
                for t in range(NT):
                    o = (hd % 2) * T + t * P
                    mm(ps[:, hd // 2, o:o + P], vs[t], am[:, hd, t, :], start=True, stop=False)
                    last = mm(ps[:, hd // 2, o:o + P], vs[1 - t], off[:, 1 - t, hd, :], start=False, stop=True)
            last.then_inc(av, 1)
            pe.wait_ge(o2_ok, 1)
            for a in range(H * NT):
                last = mm(ps[:, 6, a:a + 1], wk[:, 1, a // NT, (a % NT) * P:(a % NT + 1) * P], ones_v[:, 0:1],
                          start=True, stop=True)
            last.then_inc(oms_ps, 1)
            pe.wait_ge(orec_ok, 1)
            for a in range(H * NT):
                last = mm(ps[:, 6 + a // 4, (a % 4) * P:(a % 4 + 1) * P], orms[:, 8 + a:9 + a].to_broadcast([P, P]),
                          ident, start=True, stop=True)
            last.then_inc(obc_ps, 1)

            def out_part(t, half, lo, hi):
                for c in range(lo, hi):
                    last = mm(ps[:, (4, 2)[half] + t, :], cat[:, c, t * P:(t + 1) * P],
                              ring[:, (N_IN + half) % SLOTS, c, :], start=(c == 4), stop=(c == 3))
                return last

            pe.wait_ge(catb_ok, 1)
            for half in range(2):
                pe.wait_ge(full[(N_IN + half) % SLOTS], 32)
                for t in range(NT):
                    out_part(t, half, 4, 8)
            pe.wait_ge(cata_ok, 1)
            for t in range(NT):
                for half in range(2):
                    last = out_part(t, half, 0, 4)
                    last.then_inc(oproj, 1)
            pe.wait_ge(r_in, 32)
            for t in range(NT):
                pe.wait_ge(n2_ok, t + 1)
                for c in range(C):
                    last = tr(ps[:, 6 * t + c // 4, (c % 4) * P:(c % 4 + 1) * P], n2[:, t, c * P:(c + 1) * P], ident)
                last.then_inc(n2T_ps, 1)
            pe.wait_ge(h_ok, NT)
            for t in range(NT):
                pe.wait_ge(n2T_sb, t + 1)
                pe.wait_ge(n2T_dve, t + 1)
                o = ps[:, 3, t * E:(t + 1) * E]
                for c in range(C):
                    mm(o, nT[:, c, t * P:(t + 1) * P], rw[:, c, :], start=(c == 0), stop=False)
                last = mm(o, ones[0:1, 0:P], rb[:], start=False, stop=True)
            last.then_inc(lgt_ps, 1)
            pe.wait_ge(sel_ok, 1)
            s = rt[:, 7]
            mm(ps[:, 3, 64:64 + E], tri, s[:, 0, :], start=True, stop=True)
            mm(ps[:, 3, 96:96 + E], tri, s[:, 1, :], start=True, stop=False)
            mm(ps[:, 3, 96:96 + E], ones[:, 0:P], s[:, 0, :], start=False, stop=True)
            mm(ps[:, 3, P:P + E], ones[:, 0:P], s[:, 0, :], start=True, stop=False)
            mm(ps[:, 3, P:P + E], ones[:, 0:P], s[:, 1, :], start=False, stop=True).then_inc(rank_ps, 1)
            pe.wait_ge(gates_ok, 1)
            for t in range(NT):
                last = tr(ps[0:E, 2, T + t * P:T + (t + 1) * P], gates[:, t, :], ident)
            last.then_inc(gT_ps, 1)
            def gather(n, part):
                pe.wait_ge(s_sel, n + 1)
                for c in range(4 * part, 4 * part + 4):
                    for t in range(NT):
                        last = mm(ps[:, 3, c * BLK:(c + 1) * BLK], n2[:, t, c * P:(c + 1) * P], sel[:, t, :],
                                  start=(t == 0), stop=(t == NT - 1))
                if part == 1:
                    last.then_inc(s_xps, 1)

            def multiply(n, uu):
                j, half = ORDER[uu]
                if half == 0:
                    if not (isinstance(n, int) and n == 0 and j < 2):
                        pe.wait_ge(s_ev, N_EXP * n + j - 1)
                    if j == 0:
                        pe.wait_ge(s_xl, n + 1)
                if j >= 4:
                    pe.wait_ge(s_al, 2 * n + half + 1)
                lhs = xg if j < 4 else aT
                for part, src, ready in ((0, wh, s_wh), (1, wl, s_wl)):
                    pe.wait_ge(ready, UNITS * n + uu + 1)
                    for c in range(4):
                        last = mm(ps[:, j % 2, :], lhs[:, 4 * half + c, :], src[:, uu % WD, c, :],
                                  start=(half == 0 and part == 0 and c == 0),
                                  stop=(half == 1 and part == 1 and c == 3))
                last.then_inc(s_mm, 1)

            def transpose_sum(n, j):
                pe.wait_ge(s_ev, N_EXP * n + j + 1)
                if j == 0 and not (isinstance(n, int) and n == 0):
                    pe.wait_ge(s_pre, 2 * n)
                if j == 2:
                    pe.wait_ge(s_pre, 2 * n + 1)
                for c in range(4):
                    o = (j % 2) * 4 * BLK + c * BLK
                    last = mm(ps[:, 2, o:o + BLK], hid[:, j % 2, c * P:(c + 1) * P], ident2, start=True, stop=True)
                last.then_inc(s_tr, 1)

            def gates_to_rows(n):
                pe.wait_ge(s_selg, n + 1)
                pe.wait_ge(s_xl, n + 1)
                for t in range(NT):
                    last = tr(ps[:, 3, t * P:(t + 1) * P], selg[:, t].rearrange("p a b -> p (a b)"), ident)
                last.then_inc(s_gps, 1)

            def combine(n, piece):
                if piece == 0:
                    pe.wait_ge(s_gt, n + 1)
                    pe.wait_ge(s_ev, N_EXP * n + 6)
                t, half = piece // 2, piece % 2
                mm(ps[:, 4 + piece, :], gsel[:, t, :], y[:, half * CW:(half + 1) * CW],
                   start=False, stop=True, skip_group_check=True).then_inc(s_comb, 1)

            def body(n, before, following):
                for uu in range(UNITS):
                    multiply(n, uu)
                    if uu == 1 and before:
                        gates_to_rows(n - 1)
                    if uu == 2:
                        transpose_sum(n, 0)
                    if uu == 4:
                        transpose_sum(n, 1)
                    if uu == 5:
                        if before:
                            combine(n - 1, 0)
                        if following:
                            gather(n + 1, 0)
                    if uu == 6:
                        transpose_sum(n, 2)
                        if following:
                            gather(n + 1, 1)
                    if uu == 7:
                        if before:
                            combine(n - 1, 1)
                        transpose_sum(n, 3)
                    if uu == 8 and before:
                        combine(n - 1, 2)
                        combine(n - 1, 3)

            def finish(n):
                gates_to_rows(n)
                for piece in range(NPC):
                    combine(n, piece)

            gather(0, 0)
            gather(0, 1)
            pe.wait_ge(gT_sb, 1)
            pe.wait_ge(b2_in, 16)
            for t in range(NT):
                for half in range(2):
                    last = mm(ps[:, 4 + 2 * t + half, :], gT[:, t * P:(t + 1) * P],
                              b2_rows[:, half * CW:(half + 1) * CW], start=True, stop=True)
            last.then_inc(acc0, 1)
            body(0, False, True)
            with pe.Fori(1, E - 1) as n:
                body(n, True, True)
            body(E - 1, True, False)
            finish(E - 1)
            pe.wait_ge(tabled, 1)
            n_more = pe.value_load(nextra[0:1, 0:1], min_val=0, max_val=EXTRA)
            with pe.Fori(0, EXTRA) as i:
                with pe.If(i < n_more):
                    gather(E + i, 0)
                    gather(E + i, 1)
                    body(E + i, False, False)
                    finish(E + i)
                pe.nop()
            tr(ps[:, 2, 0:P], ident, ident).then_inc(y_all, 1)


def constants():
    import numpy as np
    c = np.zeros((P, K_END), np.float32)
    c[:, K_ID:K_ID + P] = np.eye(P)
    c[:, K_ID2:K_ID2 + BLK] = np.tile(np.eye(BLK), (2, 1))
    c[:, K_IOTA:K_IOTA + T] = np.arange(T)
    s, t = np.arange(P)[:, None], np.arange(P)[None, :]
    c[:, K_TRI:K_TRI + P] = s < t
    m = np.zeros((P, 2 * len(LEVELS) + 1, P), np.float32)
    for i, h in enumerate(LEVELS):
        m[:, i, :] = (s // (2 * h) == t // (2 * h)) & (s % (2 * h) < h) & (t % (2 * h) >= h)
        m[:, len(LEVELS) + i, :] = m[:, i, :].T
    m[:, 2 * len(LEVELS), :] = s == t
    return c, m


def kernel(x, norm1_w, w_in, lb_logits, hgrn_norm_w, dw_w, dw_b, conv_ln_w, conv_ln_b,
           w_out, norm2_w, router_w, router_b, w1, b1, w2, b2, final_norm_w):
    import numpy as np
    import concourse.bacc as bacc
    from concourse.bass_utils import run_bass_kernel_spmd
    c, m = constants()
    rows = lambda a: np.asarray(a).reshape(-1, P)
    ins = {
        "x": np.asarray(x)[0], "w_in": np.asarray(w_in)[0],
        "w_out": np.asarray(w_out)[0], "w1": np.asarray(w1)[0], "w2": np.asarray(w2)[0],
        "prm": np.concatenate([rows(lb_logits), rows(dw_b), rows(conv_ln_w), rows(conv_ln_b), rows(hgrn_norm_w),
                               rows(norm1_w)]),
        "dww": rows(dw_w), "b1": np.asarray(b1)[0], "b2": np.asarray(b2)[0],
        "router_w": np.asarray(router_w)[0], "router_b": np.asarray(router_b)[0],
        "norm2_w": np.asarray(norm2_w)[0], "final_w": np.asarray(final_norm_w), "consts": c, "masks": m,
    }
    ins = {k: np.ascontiguousarray(a) for k, a in ins.items()}
    nc = bacc.Bacc("TRN2", target_bir_lowering=False, num_devices=1)
    args = {k: nc.dram_tensor("in_" + k, a.shape, mybir.dt.from_np(a.dtype), kind="ExternalInput").ap()
            for k, a in ins.items()}
    out = nc.dram_tensor("out", (T, D), F32, kind="ExternalOutput").ap()
    encoder_layer(nc, out=out, **args)
    r = run_bass_kernel_spmd(nc, [{"in_" + k: a for k, a in ins.items()}], core_ids=[0])
    return r.results[0]["out"].reshape(1, T, D)
```

```python
import concourse.bass as bass
from concourse import mybir
from contextlib import ExitStack

F32 = mybir.dt.float32
F32R = mybir.dt.float32r
I32 = mybir.dt.int32
U8 = mybir.dt.uint8
ALU = mybir.AluOpType
ACT = mybir.ActivationFunctionType
AX = mybir.AxisListType

P = 128
T = 256
NT = T // P
D = 1024
C = D // P
H = 4
CH = 4
TAPS = 31
PAD = TAPS // 2
E = 32
TOPK = 4
CW = 512
SLOTS = 6
BLK = 64
EXTRA = (T * TOPK + E * (BLK - 1)) // BLK - E
LIMIT = 7.0
ALPHA = 1.702
EPS = 1e-5

CV, CG, FF, FB, QZ, IV, GZ = range(7)
W_IN_COLUMNS = [5, 6, 1, 2, 0, 3, 4]
N_IN = 7
N_FRONT = N_IN + 2
N_EXP = 6
LEVELS = [128, 64, 32, 16, 8, 4, 2, 1]
N_MASK = len(LEVELS)
EXPS = 3
UNITS = 2 * N_EXP
ORDER = [(j, a) for j in range(4) for a in (0, 1)] + [(4, 0), (5, 0), (4, 1), (5, 1)]
DONE = [max(i for i, u in enumerate(ORDER) if u[0] == j) + 1 for j in range(N_EXP)]
NPC = 4
PRM = 40
DG = 3
WD = 3

K_ID, K_ID2, K_IOTA, K_TRI = 0, 128, 192, 448
K_END = 576


def encoder_layer(nc, x, w_in, w_out, w1, w2, prm, dww, b1, b2, router_w, router_b,
                  norm2_w, final_w, consts, masks, out):
    w_in_v = w_in.rearrange("(c p) n -> p c n", p=P)
    w_out_v = w_out.rearrange("(c p) n -> p c n", p=P)
    w1_v = w1.rearrange("e (c p) n -> e p c n", p=P)
    w2_v = w2.rearrange("e (c p) n -> e p c n", p=P)
    x_v = x.rearrange("(i p) d -> p i d", p=P)
    out_v = out.rearrange("(i p) d -> p i d", p=P)

    keep = ExitStack()
    front = ExitStack()

    def sb(name, shape, dt=F32, stack=keep):
        return stack.enter_context(nc.sbuf_tensor(name, shape, dt))

    def sem(name):
        return keep.enter_context(nc.semaphore(name))

    with keep:
        ring = sb("ring", [P, SLOTS, C, CW])
        h = sb("h", [P, NT, D])
        n2 = sb("n2", [P, NT, D])
        cst = sb("cst", [P, K_END])
        wrow = sb("wrow", [P, D])
        b1T = sb("b1T", [P, 2 * C, E])
        gates = sb("gates", [P, NT, E])
        rankm = sb("rankm", [P, NT, E])
        table = sb("table", [1, 2, 16], I32)
        nextra = sb("nextra", [1, 1], I32)
        eps = sb("eps", [P, 1])
        ones = sb("ones", [P, T])
        ones_v = sb("ones_v", [P, P])
        ones_c = sb("ones_c", [P, P])
        ssum = sb("ssum", [P, 8])
        ident = cst[:, K_ID:K_ID + P]
        ident2 = cst[:, K_ID2:K_ID2 + BLK]
        iota = cst[:, K_IOTA:K_IOTA + T]
        tri = cst[:, K_TRI:K_TRI + P]

        nT = sb("nT", [P, C, T], stack=front)
        msk = sb("msk", [P, N_MASK, P], U8, front)
        q = sb("q", [P, H, T], stack=front)
        kf = sb("kf", [P, H, T], stack=front)
        kb = sb("kb", [P, H, T], stack=front)
        bf = sb("bf", [P, H, T], stack=front)
        bb = sb("bb", [P, H, T + 1], stack=front)
        cv = sb("cv", [P, CH, T], stack=front)
        u = sb("u", [P, CH, T + 2 * PAD], stack=front)
        acc = sb("acc", [P, CH, T], stack=front)
        ex = sb("ex", [P, EXPS, H, T], stack=front)
        wk = sb("wk", [P, 2, 2, H, T], stack=front)
        am = sb("am", [P, H, NT, P], stack=front)
        cat = sb("cat", [P, C, T], stack=front)
        dwT = sb("dwT", [P, TAPS * CH], stack=front)
        prmT = sb("prmT", [P, PRM], stack=front)
        n1w = prmT[:, 32:32 + C]
        rw = sb("rw", [P, C, E], stack=front)
        rb = sb("rb", [1, E], stack=front)
        lbs = sb("lbs", [P, 6, 2, H], stack=front)
        orms = sb("orms", [P, 16], stack=front)
        lg = sb("lg", [P, NT, E], stack=front)
        mx = sb("mx", [P, NT, 8], stack=front)
        sm = sb("sm", [P, 8, NT], stack=front)
        flat = "p h t -> p (h t)"
        rt = bf[:].rearrange(flat)[:, 0:8 * NT * E].rearrange("p (k i e) -> p k i e", k=8, i=NT)
        msk_f = ex[:, 0].rearrange(flat).rearrange("p (m t) -> p m t", t=P)
        v = cv[:].rearrange(flat).rearrange("p (i e) -> p i e", i=NT)
        gate = nT[:, 0:4, :]
        junk = wk[:].rearrange("p a b h t -> p (a b h t)")[:, 0:NT * D].rearrange("p (i d) -> p i d", i=NT)
        sA = cat[:, 0:4, :]
        sB = cat[:, 4:8, :]
        b1_rows = n2[0:E].rearrange("p a b -> p (a b)")
        off = n2[:, 0, :].rearrange("p (d h t) -> p d h t", d=2, h=H)
        tapped = am[:].rearrange("p h i t -> p h (i t)")
        rows = u[:, 0, 0:256].rearrange("p (a b) -> p a b", b=P)
        front.close()

        wh = sb("wh", [P, WD, 4, CW], F32R)
        wl = sb("wl", [P, WD, 4, CW], F32R)
        xg = sb("xg", [P, C, 2 * BLK], F32R)
        aT = sb("aT", [P, C, 2 * BLK], F32R)
        hid = sb("hid", [P, 2, CW])
        y = sb("y", [P, D])
        pre = sb("pre", [P, 2, 4, BLK])
        glu = sb("glu", [P, 4, BLK])
        lin = sb("lin", [P, 4, BLK])
        sig = sb("sig", [P, 4, BLK])
        gs = sb("gs", [P, 4, BLK])
        act_ = sb("act_", [P, 4, BLK])
        sel = sb("sel", [P, NT, BLK])
        selg = sb("selg", [P, NT, 2, BLK])
        gsel = sb("gsel", [P, NT, P])
        cur = sb("cur", [P, 4, NT])

        gT = sb("gT", [E, T])
        b2_rows = sb("b2_rows", [E, D])
        ctf = sb("ctf", [1, 3, E])
        cmp_ = sb("cmp_", [1, 2, EXTRA, E])
        eb = sb("eb", [1, 4, 16])

        ps = keep.enter_context(nc.psum_tensor("ps", [P, 8, 512], F32))

        def pair(i):
            return ps[:, 2 * i:2 * i + 2, :].rearrange("p a b -> p (a b)")

        def heads(ap):
            return ap.rearrange("p (h t) -> p h t", h=4)

        full = [[sem(f"ring_full{s}_{half}") for half in (0, 1)] for s in range(SLOTS)]
        x_in = [sem(f"x_in{t}") for t in range(NT)]
        c_in, m_in, p_in, b1_in, b2_in, w2r_in, fw_in, r_in = [sem(n) for n in (
            "consts_in", "masks_in", "params_in", "b1_in", "b2_in",
            "norm2_in", "final_in", "router_in")]
        (fills, rms1, xn_ok, xT_ok, nT_act, nT_dve, prm_ps, prm_sb, proj, ev_act, ev_dve,
         f_ok, logf_ok, sc_ok, e_ok, exp_ok, w_ok, prod, lev) = [sem(n) for n in (
             "fills", "rms1", "xn_ready", "xT_in_psum", "nT_by_act", "nT_by_dve",
             "params_in_psum", "params_ready", "projected", "evacuated_by_act", "evacuated_by_dve",
             "gate_ready", "log_gate_ready", "prefix_ready", "exponents_ready", "exps_ready",
             "scaled_ready", "level_products", "levels_merged")]
        (conv_ok, mu_ps, xc_ok, xc2_ok, var_ps, std_ok, ln_ok, lsg_ok, catb_ok) = [sem(n) for n in (
            "conv_ready", "conv_mean", "conv_centred", "conv_squares", "conv_var",
            "conv_std", "conv_normed", "conv_sigmoid", "cat_conv_ready")]
        (av, o2_ok, oms_ps, ostd_ok, cata_ok, oproj, h_ok, rms2, n2_ok, n2T_ps, n2T_sb,
         lgt_ps, lg_ok, ex4_ok, sel_ok, rank_ps, gates_ok, gT_ps, gT_sb, routed) = [sem(n) for n in (
             "attended", "o_squares", "o_mean_square", "o_rms", "cat_heads_ready",
             "out_projected", "h_ready", "rms2", "n2_ready", "n2T_in_psum", "n2T_ready",
             "logits_in_psum", "logits_ready", "gate_exps", "chosen_ready", "ranks_in_psum",
             "gates_ready", "gatesT_in_psum", "gatesT_ready", "routed")]
        (s_sel, s_selg, s_xps, s_xh, s_xl, s_wh, s_wl, s_wp, s_mm, s_ev, s_tr, s_pre, s_glu, s_sig, s_gs,
         s_act, s_ah, s_al, s_gps, s_gt, s_comb, s_cur, s_lin) = [sem(n) for n in (
             "block_chosen", "block_gates", "gathered", "x_high", "x_low", "w_high", "w_low", "w_low_rest",
             "unit_multiplied", "chunk_evacuated", "hidden_transposed", "bias_added", "clamped",
             "sigmoid_ready", "gated_ready", "act_ready", "act_high", "act_low", "block_gatesT",
             "block_gatesT_ready", "combined", "columns_copied", "linear_clamped")]
        dve_seq, act_seq = sem("dve_seq"), sem("act_seq")
        (y_all, rms3, y_ok, y_out, n2T_dve, msk_ok, tabled, tap_ok, tap_sum, orec_ok, obc_ps, obc_ok) = [
            sem(n) for n in (
                "experts_done", "rms3", "y_ready", "y_stored", "n2T_by_dve", "masks_ready", "extra_blocks_ready",
                "taps_multiplied", "taps_summed", "o_reciprocals", "o_scales_in_psum", "o_scales_ready")]

        def slot_of(j):
            return (N_FRONT + j) % SLOTS

        def filled(eng, n, j, half):
            eng.wait_ge(full[slot_of(j)][half], 16 * (n + (N_FRONT + j) // SLOTS + 1))

        def level_views(ap, hh):
            a = ap.rearrange("p h (n two j) -> p h n two j", two=2, j=hh)
            return a[:, :, :, 0, :], a[:, :, :, 1, :]

        N_STEP = 1 + len(LEVELS)
        block = keep.enter_context(nc.Block())

        @block.sync
        def _(sp):
            for t in range(NT):
                sp.dma_start(h[:, t, :], x_v[:, t, :]).then_inc(x_in[t], 16)
            sp.dma_start(cst[:], consts).then_inc(c_in, 16)
            sp.dma_start(rows[0:TAPS * CH, 0, :], dww).then_inc(p_in, 16)
            sp.dma_start(rows[0:PRM, 1, :], prm).then_inc(p_in, 16)

            def load_half(slot, src, half):
                part = slice(4 * half, 4 * half + 4)
                sp.dma_start(ring[:, slot, part, :], src[:, part, :]).then_inc(full[slot][half], 16)

            def load(slot, src):
                for half in (0, 1):
                    load_half(slot, src, half)

            for i, col in enumerate(W_IN_COLUMNS):
                if i >= SLOTS:
                    sp.wait_ge(proj, i - SLOTS + 1)
                load(i % SLOTS, w_in_v[:, :, col * CW:(col + 1) * CW])
            for i in range(2):
                sp.wait_ge(proj, N_IN + i - SLOTS + 1)
                load((N_IN + i) % SLOTS, w_out_v[:, :, i * CW:(i + 1) * CW])

            def load_unit(e, j, half):
                if j < 4:
                    lo = (j // 2) * CW + (j % 2) * D
                    src = w1_v[e, :, :, lo:lo + CW]
                else:
                    src = w2_v[e, :, :, (j - 4) * CW:(j - 3) * CW]
                load_half(slot_of(j), src, half)

            def block_units(n, e):
                for uu, (j, half) in enumerate(ORDER):
                    sp.wait_ge(s_wl, UNITS * (n - 1) + uu + 1)
                    sp.wait_ge(s_wp, UNITS * (n - 1) + uu + 1)
                    load_unit(e, j, half)

            for j, half in ORDER:
                if half == 0 and j < 4:
                    sp.wait_ge(proj, j + 4)
                if (j, half) == (4, 0):
                    sp.wait_ge(oproj, 2 * NT)
                load_unit(0, j, half)
            with sp.Fori(1, E) as e:
                block_units(e, e)
            sp.wait_ge(tabled, 1)
            n_more = sp.value_load(nextra[0:1, 0:1], min_val=0, max_val=EXTRA)
            with sp.If(n_more > 0):
                with sp.Fori(0, EXTRA) as i:
                    with sp.If(i < n_more):
                        e = sp.value_load(table[0:1, 0, bass.ds(i, 1)], min_val=0, max_val=E - 1)
                        block_units(E + i, e)
                    sp.nop()
            sp.wait_ge(y_ok, 1)
            sp.dma_start(out_v[:, 0, :], h[:, 0, :]).then_inc(y_out, 16)
            sp.wait_ge(y_ok, 2)
            sp.dma_start(out_v[:, 1, :], h[:, 1, :]).then_inc(y_out, 16)
            sp.wait_ge(y_out, 32)

        @block.gpsimd
        def _(pool):
            g = nc.gpsimd
            g.memset(eps[:], EPS).then_inc(fills, 1)
            g.memset(ones[:], 1.0).then_inc(fills, 1)
            g.memset(ones_v[:], 1.0 / P).then_inc(fills, 1)
            g.memset(ones_c[:], 1.0 / CW).then_inc(fills, 1)
            g.memset(bb[:, :, 0:1], 0.0).then_inc(fills, 1)
            pool.wait_ge(prm_sb, 2)
            g.memset(u[:, :, 0:PAD], 0.0).then_inc(fills, 1)
            g.memset(u[:, :, PAD + T:], 0.0).then_inc(fills, 1)
            pool.wait_ge(m_in, 16)
            g.tensor_copy(msk[:], msk_f).then_inc(msk_ok, 1)
            for tap in range(1, TAPS):
                pool.wait_ge(tap_ok, tap + 1)
                if tap > 1:
                    pool.wait_ge(tap_sum, tap - 1)
                g.tensor_tensor(acc[:, 3, :], acc[:, 3, :], tapped[:, tap % 4, :], ALU.add).then_inc(tap_sum, 1)
            pool.wait_ge(tap_sum, TAPS - 1)
            g.memset(am[:], 0.0).then_inc(fills, 1)
            pool.wait_ge(f_ok, 4)
            g.tensor_tensor(wk[:, 0, 0], kf[:], kb[:], ALU.add).then_inc(w_ok, 1)
            for k in range(1, N_STEP):
                if k >= 2:
                    pool.wait_ge(prod, k - 1)
                for d in (0, 1):
                    m = 2 * (k - 1) + d
                    pool.wait_ge(exp_ok, m + 1)
                    e_half = level_views(ex[:, m % EXPS], LEVELS[k - 1])
                    keys = level_views((kf, kb)[d][:], LEVELS[k - 1])
                    queries = level_views(q[:], LEVELS[k - 1])
                    scaled_k = level_views(wk[:, k % 2, 0], LEVELS[k - 1])
                    scaled_q = level_views(wk[:, k % 2, 1], LEVELS[k - 1])
                    g.tensor_tensor(scaled_k[d], keys[d], e_half[d], ALU.mult)
                    if m == 0:
                        pool.wait_ge(ev_dve, 2)
                    g.tensor_tensor(scaled_q[1 - d], queries[1 - d], e_half[1 - d], ALU.mult).then_inc(w_ok, 1)

            def choose_gates(n, e):
                g.tensor_copy(cur[:, 1, :], gates[:, :, bass.ds(e, 1)].rearrange("p a b -> p (a b)"))\
                 .then_inc(s_cur, 1)
                if not (isinstance(n, int) and n == 0):
                    pool.wait_ge(s_gps, n)
                pool.wait_ge(s_cur, n + 1)
                pool.wait_ge(s_sel, n + 1)
                for t in range(NT):
                    last = g.tensor_tensor(selg[:, t], sel[:, t:t + 1, :].to_broadcast([P, 2, BLK]),
                                           cur[:, 1, t:t + 1].unsqueeze(2).to_broadcast([P, 2, BLK]), ALU.mult)
                last.then_inc(s_selg, 1)

            def gated(n, hf):
                pool.wait_ge(s_glu, 2 * n + hf + 1)
                pool.wait_ge(s_sig, 2 * n + hf + 1)
                g.tensor_tensor(gs[:], glu[:], sig[:], ALU.mult).then_inc(s_gs, 1)

            def split_low(n, uu):
                pool.wait_ge(s_wh, UNITS * n + uu + 1)
                if not (isinstance(n, int) and UNITS * n + uu < WD):
                    pool.wait_ge(s_mm, UNITS * n + uu + 1 - WD)
                j, half = ORDER[uu]
                g.tensor_tensor(wl[:, uu % WD, DG:4], ring[:, slot_of(j), 4 * half + DG:4 * half + 4, :],
                                wh[:, uu % WD, DG:4].bitcast(F32), ALU.subtract).then_inc(s_wp, 1)

            def body(n, e):
                for uu in range(UNITS):
                    split_low(n, uu)
                    if uu == 1:
                        choose_gates(n, e)
                    if uu == 8:
                        gated(n, 0)
                    if uu == 9:
                        gated(n, 1)

            pool.wait_ge(routed, 1)
            body(0, 0)
            with pool.Fori(1, E) as e:
                body(e, e)
            pool.wait_ge(tabled, 1)
            n_more = pool.value_load(nextra[0:1, 0:1], min_val=0, max_val=EXTRA)
            with pool.If(n_more > 0):
                with pool.Fori(0, EXTRA) as i:
                    with pool.If(i < n_more):
                        e = pool.value_load(table[0:1, 0, bass.ds(i, 1)], min_val=0, max_val=E - 1)
                        body(E + i, e)
                    pool.nop()

        @block.scalar
        def _(act):
            a = nc.scalar
            act.dma_start(wrow[:], norm2_w.partition_broadcast(P)).then_inc(w2r_in, 16)
            act.dma_start(rw[:], router_w.rearrange("(c p) e -> p c e", p=P)).then_inc(r_in, 16)
            act.dma_start(rb[:], router_b.rearrange("(a e) -> a e", a=1)).then_inc(r_in, 16)

            step = [0]

            def link(ins):
                step[0] += 1
                ins.then_inc(act_seq, 1)
                act.wait_ge(act_seq, step[0])

            act.wait_ge(fills, 1)
            a.activation(ssum[:, 6:7], eps[:], ACT.Sqrt)
            for t in range(NT):
                act.wait_ge(x_in[t], 16)
                last = a.activation(junk[:, t, :], h[:, t, :], ACT.Square,
                                    accum_out=ssum[:, t:t + 1])
            link(last)
            a.activation(ssum[:, 2:4], ssum[:, 0:2], ACT.Sqrt, bias=eps[:], scale=1.0 / D).then_inc(rms1, 1)
            act.dma_start(msk_f, masks).then_inc(m_in, 16)
            act.wait_ge(prm_sb, 2)
            for c in range(C // 2):
                act.wait_ge(xT_ok, c // 2 + 1)
                a.activation(nT[:, c, :], ps[:, 4 + c // 2, (c % 2) * T:(c % 2 + 1) * T], ACT.Copy, scale=n1w[:, c:c + 1])\
                 .then_inc(nT_act, 1)
            act.wait_ge(xT_ok, C // 2)
            act.dma_start(b1_rows, b1).then_inc(b1_in, 16)
            act.wait_ge(sc_ok, 1)
            a.activation(lbs[:, 2:4], lbs[:, 0:2], ACT.Exp).then_inc(sc_ok, 1)

            def exps(k):
                act.wait_ge(e_ok, k + 1)
                a.activation(ex[:, k % EXPS], ex[:, k % EXPS], ACT.Exp).then_inc(exp_ok, 1)

            def tap_products(lo, hi):
                for tap in range(lo, hi):
                    wt = dwT[:, tap * CH + 3:tap * CH + 4]
                    if tap == 0:
                        a.activation(acc[:, 3, :], u[:, 3, 0:T], ACT.Identity, scale=wt, bias=prmT[:, 19:20])\
                         .then_inc(tap_ok, 1)
                        continue
                    if tap > 4:
                        act.wait_ge(tap_sum, tap - 4)
                    a.activation(tapped[:, tap % 4, :], u[:, 3, tap:tap + T], ACT.Copy, scale=wt).then_inc(tap_ok, 1)

            act.wait_ge(proj, CV + 1)
            a.activation(cv[:], heads(pair(CV % 2)), ACT.Copy).then_inc(ev_act, 1)
            act.wait_ge(proj, CG + 1)
            a.activation(sA, heads(pair(CG % 2)), ACT.Sigmoid).then_inc(ev_act, 1)
            act.wait_ge(ev_dve, 1)
            tap_products(0, 16)
            act.wait_ge(proj, FF + 1)
            a.activation(sB, heads(pair(FF % 2)), ACT.Sigmoid).then_inc(ev_act, 1)
            act.wait_ge(f_ok, 2)
            a.activation(sB, sB, ACT.Ln).then_inc(logf_ok, 1)
            tap_products(16, TAPS)
            exps(0)
            act.wait_ge(proj, FB + 1)
            act.wait_ge(sc_ok, 3)
            a.activation(sB, heads(pair(FB % 2)), ACT.Sigmoid).then_inc(ev_act, 1)
            act.wait_ge(f_ok, 4)
            a.activation(sB, sB, ACT.Ln).then_inc(logf_ok, 1)
            exps(1)
            exps(2)
            act.wait_ge(proj, QZ + 1)
            a.activation(sA, heads(pair(QZ % 2)), ACT.Sigmoid).then_inc(ev_act, 1)
            for k in range(3, 7):
                exps(k)
            act.wait_ge(proj, IV + 1)
            a.activation(v, pair(IV % 2).rearrange("p (t e) -> p t e", t=NT), ACT.Copy).then_inc(ev_act, 1)
            for k in range(7, 11):
                exps(k)
            act.wait_ge(xc_ok, 1)
            a.activation(u[:, :, 0:T], acc[:], ACT.Square).then_inc(xc2_ok, 1)
            for k in range(11, 15):
                exps(k)
            act.wait_ge(var_ps, 1)
            a.activation(u[:, 0, 0:T], ps[:, 3, T:2 * T], ACT.Sqrt, bias=eps[:]).then_inc(std_ok, 1)
            exps(15)
            act.wait_ge(ln_ok, 1)
            for c in range(CH):
                last = a.activation(u[:, c, 0:T], acc[:, c, :], ACT.Sigmoid,
                                    scale=prmT[:, 20 + c:21 + c], bias=prmT[:, 24 + c:25 + c])
            last.then_inc(lsg_ok, 1)
            act.wait_ge(proj, GZ + 1)
            a.activation(sA, heads(pair(GZ % 2)), ACT.Sigmoid).then_inc(ev_act, 1)
            act.wait_ge(av, 1)
            a.activation(wk[:, 1, 0], heads(pair(0)), ACT.Square).then_inc(o2_ok, 1)
            act.wait_ge(oms_ps, 1)
            a.activation(orms[:, 0:8], ps[:, 6, 0:8], ACT.Sqrt, bias=eps[:]).then_inc(ostd_ok, 1)
            act.wait_ge(obc_ps, 1)
            a.activation(ex[:, 0], heads(pair(3)), ACT.Copy).then_inc(obc_ok, 1)
            def n2_to_columns(t):
                act.wait_ge(n2T_ps, t + 1)
                a.activation(nT[:, 0:4, t * P:(t + 1) * P], ps[:, 6 * t, :].rearrange("p (c t) -> p c t", c=4), ACT.Copy)\
                 .then_inc(n2T_sb, 1)

            for t in range(NT):
                act.wait_ge(h_ok, t + 1)
                link(a.activation(junk[:, t, :], h[:, t, :], ACT.Square, accum_out=ssum[:, t:t + 1]))
                a.activation(ssum[:, 2 + t:3 + t], ssum[:, t:t + 1], ACT.Sqrt, bias=eps[:], scale=1.0 / D)\
                 .then_inc(rms2, 1)
                if t == 0:
                    n2_to_columns(0)
            act.dma_start(b2_rows[:], b2).then_inc(b2_in, 16)
            n2_to_columns(1)
            act.dma_start(wrow[:], final_w.partition_broadcast(P)).then_inc(fw_in, 16)
            act.wait_ge(lg_ok, 1)
            act.wait_ge(lgt_ps, NT)
            for t in range(NT):
                last = a.activation(rt[:, 0, t, :], lg[:, t, :], ACT.Exp, bias=sm[:, 0, t:t + 1])
            last.then_inc(ex4_ok, 1)
            def split_high(n, uu):
                j, half = ORDER[uu]
                filled(act, n, j, half)
                if not (isinstance(n, int) and UNITS * n + uu < WD):
                    act.wait_ge(s_mm, UNITS * n + uu + 1 - WD)
                a.activation(wh[:, uu % WD], ring[:, slot_of(j), 4 * half:4 * half + 4, :], ACT.Copy)\
                 .then_inc(s_wh, 1)

            def evacuate(n, j):
                act.wait_ge(s_mm, UNITS * n + DONE[j])
                if j < 4:
                    if j >= 2:
                        act.wait_ge(s_tr, 4 * n + j - 1)
                    dst = hid[:, j % 2, :]
                else:
                    dst = y[:, (j - 4) * CW:(j - 3) * CW]
                a.activation(dst, ps[:, j % 2, :], ACT.Copy).then_inc(s_ev, 1)

            def x_high(n):
                act.wait_ge(s_xps, n + 1)
                if not (isinstance(n, int) and n == 0):
                    act.wait_ge(s_mm, UNITS * (n - 1) + DONE[3])
                a.activation(xg[:, :, 0:BLK], ps[:, 3, :].rearrange("p (c s) -> p c s", c=C), ACT.Copy)\
                 .then_inc(s_xh, 1)

            def gates_out(n):
                act.wait_ge(s_gps, n + 1)
                a.activation(gsel[:], ps[:, 3, 0:T].rearrange("p (i t) -> p i t", i=NT), ACT.Copy).then_inc(s_gt, 1)

            def sigmoid(n, hf):
                act.wait_ge(s_glu, 2 * n + hf + 1)
                a.activation(sig[:], glu[:], ACT.Sigmoid, scale=ALPHA).then_inc(s_sig, 1)

            def a_high(n, hf):
                act.wait_ge(s_act, 2 * n + hf + 1)
                a.activation(aT[:, 4 * hf:4 * hf + 4, 0:BLK], act_[:], ACT.Copy).then_inc(s_ah, 1)

            def y_out_of(n, j):
                if not (isinstance(n, int) and n == 0) and j == 4:
                    act.wait_ge(s_comb, NPC * n)
                evacuate(n, j)

            def body(n, before, following, first=0):
                for uu in range(first, UNITS):
                    split_high(n, uu)
                    if uu < 2 and before:
                        y_out_of(n - 1, 4 + uu)
                    if uu == 3:
                        evacuate(n, 0)
                    if uu == 4 and before:
                        gates_out(n - 1)
                    if uu == 5:
                        evacuate(n, 1)
                    if uu == 7:
                        evacuate(n, 2)
                    if uu == 8:
                        sigmoid(n, 0)
                        evacuate(n, 3)
                        a_high(n, 0)
                    if uu == 9:
                        sigmoid(n, 1)
                    if uu == 10:
                        if following:
                            x_high(n + 1)
                        a_high(n, 1)

            def finish(n):
                gates_out(n)
                y_out_of(n, 4)
                y_out_of(n, 5)

            split_high(0, 0)
            act.wait_ge(gT_ps, 1)
            a.activation(gT[:], ps[0:E, 0, 0:T], ACT.Copy).then_inc(gT_sb, 1)
            split_high(0, 1)
            act.wait_ge(routed, 1)
            split_high(0, 2)
            x_high(0)
            body(0, False, True, 3)
            with act.Fori(1, E - 1) as n:
                body(n, True, True)
            body(E - 1, True, False)
            finish(E - 1)
            act.wait_ge(tabled, 1)
            n_more = act.value_load(nextra[0:1, 0:1], min_val=0, max_val=EXTRA)
            with act.If(n_more > 0):
                with act.Fori(0, EXTRA) as i:
                    with act.If(i < n_more):
                        x_high(E + i)
                        body(E + i, False, False)
                        finish(E + i)
                    act.nop()
            a.activation(ssum[:, 6:7], eps[:], ACT.Sqrt)
            act.wait_ge(y_all, 1)
            for t in range(NT):
                link(a.activation(n2[:, t, :], pair(2 + t), ACT.Square, accum_out=ssum[:, t:t + 1]))
                a.activation(ssum[:, 2 + t:3 + t], ssum[:, t:t + 1], ACT.Sqrt, bias=eps[:], scale=1.0 / D)\
                 .then_inc(rms3, 1)

        @block.vector
        def _(dve):
            w = nc.vector
            step = [0]

            def link(ins):
                step[0] += 1
                ins.then_inc(dve_seq, 1)
                dve.wait_ge(dve_seq, step[0])

            dve.wait_ge(rms1, 1)
            link(w.reciprocal(ssum[:, 4:6], ssum[:, 2:4]))
            for t in range(NT):
                w.tensor_scalar(n2[:, t, :], h[:, t, :], ssum[:, 4 + t:5 + t], None, ALU.mult).then_inc(xn_ok, 1)
            dve.wait_ge(prm_ps, 1)
            w.tensor_copy(dwT[:], ps[:, 0, 0:TAPS * CH])
            w.tensor_copy(prmT[:], ps[:, 0, P:P + PRM]).then_inc(prm_sb, 2)
            dve.wait_ge(prm_sb, 2)
            for c in range(C // 2, C):
                dve.wait_ge(xT_ok, c // 2 + 1)
                w.tensor_scalar(nT[:, c, :], ps[:, 4 + c // 2, (c % 2) * T:(c % 2 + 1) * T], n1w[:, c:c + 1],
                                None, ALU.mult)\
                 .then_inc(nT_dve, 1)
            lbv = prmT[:, 0:16].rearrange("p (d r h) -> p r d h", d=2, r=2)
            link(w.tensor_tensor(lbs[:, 4], lbv[:, 0], lbv[:, 1], ALU.max))
            w.tensor_tensor(lbs[:, 0], lbv[:, 0], lbs[:, 4], ALU.subtract)
            w.tensor_tensor(lbs[:, 1], lbv[:, 1], lbs[:, 4], ALU.subtract).then_inc(sc_ok, 1)
            dve.wait_ge(sc_ok, 2)
            link(w.tensor_tensor(lbs[:, 4], lbs[:, 2], lbs[:, 3], ALU.add))
            link(w.reciprocal(lbs[:, 5], lbs[:, 4]))
            link(w.tensor_tensor(lbs[:, 0], lbs[:, 2], lbs[:, 5], ALU.mult))
            link(w.tensor_scalar(lbs[:, 1], lbs[:, 0], -1.0, 1.0, ALU.mult, ALU.add))

            def conv(lo, hi):
                for tap in range(lo, hi):
                    for c in range(CH - 1):
                        wt = dwT[:, tap * CH + c:tap * CH + c + 1]
                        if tap == 0:
                            ins = w.tensor_scalar(acc[:, c, :], u[:, c, 0:T], wt, prmT[:, 16 + c:17 + c],
                                                  ALU.mult, ALU.add)
                        else:
                            dve.wait_ge(conv_ok, (tap - 1) * (CH - 1) + c + 1)
                            ins = w.scalar_tensor_tensor(out=acc[:, c, :], in0=u[:, c, tap:tap + T], scalar=wt,
                                                         in1=acc[:, c, :], op0=ALU.mult, op1=ALU.add)
                        ins.then_inc(conv_ok, 1)

            def gates_of(d):
                dve.wait_ge(ev_act, (FF, FB)[d] + 1)
                for hd in range(H):
                    last = w.tensor_scalar(sB[:, hd, :], sB[:, hd, :], lbs[:, 1, d, hd:hd + 1],
                                           lbs[:, 0, d, hd:hd + 1], ALU.mult, ALU.add)
                last.then_inc(f_ok, 1)
                dve.wait_ge(f_ok, 2 * d + 1)
                w.tensor_scalar((kf, kb)[d][:], sB, -1.0, 1.0, ALU.mult, ALU.add).then_inc(f_ok, 1)

            def prefix(d):
                dve.wait_ge(logf_ok, d + 1)
                for hd in range(H):
                    dst = bf[:, hd, :] if d == 0 else bb[:, hd, 1:T + 1]
                    last = w.tensor_tensor_scan(dst, ones[:], sB[:, hd, :], 0.0, ALU.mult, ALU.add)
                last.then_inc(sc_ok, 1)
                dve.wait_ge(sc_ok, 3 + d)

            def exponents(m):
                d, hh = m % 2, LEVELS[m // 2]
                b = bf[:] if d == 0 else bb[:, :, 0:T]
                if m >= EXPS:
                    dve.wait_ge(w_ok, m - EXPS + 2)
                first, second = level_views(b, hh)
                ea, eb_ = level_views(ex[:, m % EXPS], hh)
                mid = first[:, :, :, hh - 1:hh] if d == 0 else second[:, :, :, 0:1]
                mid = mid.to_broadcast([P, H, T // (2 * hh), hh])
                w.tensor_tensor(ea, mid, first, ALU.subtract)
                w.tensor_tensor(eb_, second, mid, ALU.subtract).then_inc(e_ok, 1)

            def merge(k):
                dve.wait_ge(prod, k + 1)
                if k == 1:
                    w.tensor_copy(off[:].rearrange("p d h t -> p (d h t)"), pair(2 + k % 2)).then_inc(lev, 1)
                    return
                if k >= 2:
                    dve.wait_ge(lev, k)
                m = max(k - 1, 0)
                mk = msk[:, m:m + 1, :].to_broadcast([P, H * NT, P])
                w.copy_predicated(am[:].rearrange("p h i t -> p (h i) t"), mk,
                                  pair(2 + k % 2).rearrange("p (a t) -> p a t", t=P)).then_inc(lev, 1)

            dve.wait_ge(fills, 7)
            dve.wait_ge(ev_act, CG + 1)
            w.tensor_tensor(u[:, :, PAD:PAD + T], cv[:], sA, ALU.mult).then_inc(ev_dve, 1)
            dve.wait_ge(ev_dve, 1)
            conv(0, 10)
            gates_of(0)
            conv(10, 12)
            prefix(0)
            dve.wait_ge(msk_ok, 1)
            exponents(0)
            dve.wait_ge(prm_ps, 2)
            w.tensor_copy(b1T[:], ps[:, 4, :].rearrange("p (c e) -> p c e", e=E)).then_inc(prm_sb, 1)
            conv(12, 17)
            gates_of(1)
            conv(17, 19)
            prefix(1)
            exponents(1)
            exponents(2)
            conv(19, 23)
            dve.wait_ge(ev_act, QZ + 1)
            w.tensor_tensor(q[:], heads(pair(QZ % 2)), sA, ALU.mult).then_inc(ev_dve, 1)
            dve.wait_ge(fills, 8)
            for k in range(N_STEP):
                if k < 4:
                    conv(23 + 2 * k, 25 + 2 * k)
                if k == 4:
                    dve.wait_ge(mu_ps, 1)
                    w.tensor_tensor(acc[:], acc[:], ps[:, 3:4, 0:T].to_broadcast([P, CH, T]), ALU.subtract)\
                     .then_inc(xc_ok, 1)
                if 2 * k + 3 < 2 * len(LEVELS):
                    exponents(2 * k + 3)
                if k == 6:
                    dve.wait_ge(std_ok, 1)
                    link(w.reciprocal(u[:, 1, 0:T], u[:, 0, 0:T]))
                    w.tensor_tensor(acc[:], acc[:], u[:, 1:2, 0:T].to_broadcast([P, CH, T]), ALU.mult)\
                     .then_inc(ln_ok, 1)
                if k == 7:
                    dve.wait_ge(lsg_ok, 1)
                    for c in range(CH):
                        last = w.tensor_scalar(acc[:, c, :], acc[:, c, :], prmT[:, 20 + c:21 + c],
                                               prmT[:, 24 + c:25 + c], ALU.mult, ALU.add)
                    link(last)
                    w.tensor_tensor(cat[:, 4:8, :], acc[:], u[:, :, 0:T], ALU.mult).then_inc(catb_ok, 1)
                if k == 8:
                    dve.wait_ge(ev_act, GZ + 1)
                    w.tensor_tensor(gate, heads(pair(GZ % 2)), sA, ALU.mult).then_inc(ev_dve, 1)
                merge(k)
                if 2 * k + 4 < 2 * len(LEVELS):
                    exponents(2 * k + 4)
            dve.wait_ge(ostd_ok, 1)
            w.reciprocal(orms[:, 8:16], orms[:, 0:8]).then_inc(orec_ok, 1)
            dve.wait_ge(obc_ok, 1)
            link(w.tensor_tensor(wk[:, 0, 0], heads(pair(0)), ex[:, 0], ALU.mult))
            for hd in range(H):
                last = w.scalar_tensor_tensor(out=cat[:, hd, :], in0=wk[:, 0, 0, hd, :], scalar=prmT[:, 28 + hd:29 + hd],
                                              in1=gate[:, hd, :], op0=ALU.mult, op1=ALU.mult)
            last.then_inc(cata_ok, 1)
            dve.wait_ge(w2r_in, 16)

            def n2_to_columns(t):
                dve.wait_ge(n2T_ps, t + 1)
                w.tensor_copy(nT[:, 4:8, t * P:(t + 1) * P], ps[:, 6 * t + 1, :].rearrange("p (c t) -> p c t", c=4))\
                 .then_inc(n2T_dve, 1)

            for t in range(NT):
                for half in range(2):
                    dve.wait_ge(oproj, 2 * t + half + 1)
                    cols = slice(half * CW, (half + 1) * CW)
                    last = w.tensor_tensor(h[:, t, cols], h[:, t, cols], ps[:, (4, 2)[half] + t, :], ALU.add)
                    if t == 1 and half == 0:
                        n2_to_columns(0)
                last.then_inc(h_ok, 1)
                dve.wait_ge(rms2, t + 1)
                link(w.reciprocal(ssum[:, 4 + t:5 + t], ssum[:, 2 + t:3 + t]))
                w.scalar_tensor_tensor(out=n2[:, t, :], in0=h[:, t, :], scalar=ssum[:, 4 + t:5 + t], in1=wrow[:],
                                       op0=ALU.mult, op1=ALU.mult).then_inc(n2_ok, 1)
            n2_to_columns(1)
            dve.wait_ge(lgt_ps, NT)
            link(w.tensor_copy(lg[:], ps[:, 2, 0:NT * E].rearrange("p (i e) -> p i e", i=NT)))
            for t in range(NT):
                last = w.max(mx[:, t, :], lg[:, t, :])
            link(last)
            w.tensor_scalar(sm[:, 0, :], mx[:, :, 0], -1.0, None, ALU.mult).then_inc(lg_ok, 1)
            v4 = mx[:, :, TOPK - 1:TOPK].to_broadcast([P, NT, E])
            w.tensor_tensor(rt[:, 1], lg[:], v4, ALU.is_gt)
            link(w.tensor_tensor(rt[:, 2], lg[:], v4, ALU.is_equal))
            w.tensor_reduce(sm[:, 1, :], rt[:, 1], AX.X, ALU.add)
            for t in range(NT):
                last = w.tensor_tensor_scan(rt[:, 3, t, :], ones[:, 0:E], rt[:, 2, t, :], 0.0, ALU.mult, ALU.add)
            link(last)
            link(w.tensor_tensor(rt[:, 4], rt[:, 3], sm[:, 1, :].unsqueeze(2).to_broadcast([P, NT, E]), ALU.add))
            link(w.tensor_scalar(rt[:, 5], rt[:, 4], float(TOPK), None, ALU.is_le))
            link(w.tensor_tensor(rt[:, 6], rt[:, 5], rt[:, 2], ALU.mult))
            w.tensor_tensor(rt[:, 7], rt[:, 6], rt[:, 1], ALU.add).then_inc(sel_ok, 1)
            dve.wait_ge(sel_ok, 1)
            dve.wait_ge(ex4_ok, 1)
            link(w.tensor_tensor(rt[:, 1], rt[:, 0], rt[:, 7], ALU.mult))
            link(w.tensor_reduce(sm[:, 2, :], rt[:, 1], AX.X, ALU.add))
            link(w.reciprocal(sm[:, 3, :], sm[:, 2, :]))
            w.tensor_tensor(gates[:], rt[:, 1], sm[:, 3, :].unsqueeze(2).to_broadcast([P, NT, E]), ALU.mult)\
             .then_inc(gates_ok, 1)
            dve.wait_ge(rank_ps, 1)
            link(w.scalar_tensor_tensor(out=rt[:, 2], in0=ps[:, 2, 64:64 + NT * E].rearrange("p (i e) -> p i e", i=NT),
                                        scalar=1.0, in1=rt[:, 7], op0=ALU.add, op1=ALU.mult))
            w.tensor_scalar(rankm[:], rt[:, 2], 1.0, None, ALU.subtract)
            w.tensor_copy(ctf[0:1, 0, :], ps[0:1, 2, P:P + E]).then_inc(routed, 1)

            def count_extra_blocks():
                link(w.tensor_scalar(ctf[0:1, 1, :], ctf[0:1, 0, :], float(BLK), None, ALU.is_gt))
                for k in range(2, T // BLK):
                    link(w.scalar_tensor_tensor(out=ctf[0:1, 1, :], in0=ctf[0:1, 0, :], scalar=float(k * BLK),
                                                in1=ctf[0:1, 1, :], op0=ALU.is_gt, op1=ALU.add))
                link(w.tensor_tensor_scan(ctf[0:1, 2, :], ones[0:1, 0:E], ctf[0:1, 1, :], 0.0, ALU.mult, ALU.add))

            def list_extra_blocks():
                jj = iota[0:1, 0:EXTRA].unsqueeze(2).to_broadcast([1, EXTRA, E])
                link(w.tensor_tensor(cmp_[0:1, 0], ctf[0:1, 2:3, :].to_broadcast([1, EXTRA, E]), jj, ALU.is_le))
                link(w.tensor_tensor(cmp_[0:1, 1], ctf[0:1, 1:2, :].to_broadcast([1, EXTRA, E]), cmp_[0:1, 0], ALU.mult))
                w.tensor_reduce(eb[0:1, 0, 0:EXTRA], cmp_[0:1, 0], AX.X, ALU.add)
                link(w.tensor_reduce(eb[0:1, 1, 0:EXTRA], cmp_[0:1, 1], AX.X, ALU.add))
                link(w.tensor_tensor(eb[0:1, 2, 0:EXTRA], iota[0:1, 0:EXTRA], eb[0:1, 1, 0:EXTRA], ALU.subtract))
                link(w.tensor_scalar(eb[0:1, 3, 0:EXTRA], eb[0:1, 2, 0:EXTRA], float(BLK), float(BLK), ALU.mult, ALU.add))
                w.tensor_scalar(table[0:1, 0, 0:EXTRA], eb[0:1, 0, 0:EXTRA], float(E - 1), None, ALU.min)
                w.tensor_scalar(table[0:1, 1, 0:EXTRA], eb[0:1, 3, 0:EXTRA], float(T - BLK), None, ALU.min)
                w.tensor_copy(nextra[:], ctf[0:1, 2, E - 1:E]).then_inc(tabled, 1)

            def split_low(n, uu):
                dve.wait_ge(s_wh, UNITS * n + uu + 1)
                if not (isinstance(n, int) and UNITS * n + uu < WD):
                    dve.wait_ge(s_mm, UNITS * n + uu + 1 - WD)
                j, half = ORDER[uu]
                w.tensor_tensor(wl[:, uu % WD, 0:DG], ring[:, slot_of(j), 4 * half:4 * half + DG, :],
                                wh[:, uu % WD, 0:DG].bitcast(F32), ALU.subtract).then_inc(s_wl, 1)

            def x_low(n):
                dve.wait_ge(s_xh, n + 1)
                w.tensor_tensor(xg[:, :, BLK:2 * BLK], ps[:, 3, :].rearrange("p (c s) -> p c s", c=C),
                                xg[:, :, 0:BLK].bitcast(F32), ALU.subtract).then_inc(s_xl, 1)

            def choose(n, e, r):
                if not (isinstance(n, int) and n == 0):
                    dve.wait_ge(s_xps, n)
                    dve.wait_ge(s_selg, n)
                for t in range(NT):
                    last = w.tensor_scalar(sel[:, t, :], iota[:, bass.ds(r, BLK)],
                                           rankm[:, t, bass.ds(e, 1)], None, ALU.is_equal)
                last.then_inc(s_sel, 1)

            def add_bias(n, e, hf):
                dve.wait_ge(s_tr, 4 * n + 2 * hf + 2)
                if not (isinstance(n, int) and n == 0 and hf == 0):
                    dve.wait_ge(s_lin, 2 * n + hf)
                bias = b1T[:, :, bass.ds(e, 1)].rearrange("p (g c) o -> p g c o", g=2)[:, :, 4 * hf:4 * hf + 4, :]
                w.tensor_tensor(pre[:], ps[:, 2, :].rearrange("p (g c s) -> p g c s", g=2, c=4),
                                bias.to_broadcast([P, 2, 4, BLK]), ALU.add).then_inc(s_pre, 1)
                dve.wait_ge(s_pre, 2 * n + hf + 1)
                if not (isinstance(n, int) and n == 0 and hf == 0):
                    dve.wait_ge(s_gs, 2 * n + hf)
                w.tensor_scalar(glu[:], pre[:, 0], LIMIT, None, ALU.min).then_inc(s_glu, 1)
                w.tensor_scalar(lin[:], pre[:, 1], LIMIT, -LIMIT, ALU.min, ALU.max).then_inc(s_lin, 1)

            def activate(n, hf):
                dve.wait_ge(s_gs, 2 * n + hf + 1)
                dve.wait_ge(s_lin, 2 * n + hf + 1)
                if not (isinstance(n, int) and n == 0 and hf == 0):
                    dve.wait_ge(s_al, 2 * n + hf)
                w.scalar_tensor_tensor(out=act_[:], in0=lin[:], scalar=1.0, in1=gs[:], op0=ALU.add, op1=ALU.mult)\
                 .then_inc(s_act, 1)

            def a_low(n, hf):
                dve.wait_ge(s_ah, 2 * n + hf + 1)
                w.tensor_tensor(aT[:, 4 * hf:4 * hf + 4, BLK:2 * BLK], act_[:],
                                aT[:, 4 * hf:4 * hf + 4, 0:BLK].bitcast(F32), ALU.subtract).then_inc(s_al, 1)

            def body(n, e, following, first=0):
                for uu in range(first, UNITS):
                    split_low(n, uu)
                    if uu == 4 and following:
                        choose(n + 1, e + 1, 0)
                    if uu == 6:
                        add_bias(n, e, 0)
                    if uu == 8:
                        activate(n, 0)
                        a_low(n, 0)
                        add_bias(n, e, 1)
                    if uu == 9:
                        activate(n, 1)
                    if uu == 10:
                        a_low(n, 1)
                    if uu == 11 and following:
                        x_low(n + 1)

            dve.wait_ge(routed, 1)
            choose(0, 0, 0)
            split_low(0, 0)
            split_low(0, 1)
            split_low(0, 2)
            x_low(0)
            count_extra_blocks()
            list_extra_blocks()
            body(0, 0, True, 3)
            with dve.Fori(1, E - 1) as n:
                body(n, n, True)
            body(E - 1, E - 1, False)
            dve.wait_ge(tabled, 1)
            n_more = dve.value_load(nextra[0:1, 0:1], min_val=0, max_val=EXTRA)
            with dve.If(n_more > 0):
                with dve.Fori(0, EXTRA) as i:
                    with dve.If(i < n_more):
                        e = dve.value_load(table[0:1, 0, bass.ds(i, 1)], min_val=0, max_val=E - 1)
                        r = dve.value_load(table[0:1, 1, bass.ds(i, 1)], min_val=0, max_val=T - BLK)
                        choose(E + i, e, r)
                        x_low(E + i)
                        body(E + i, e, False)
                    dve.nop()
            dve.wait_ge(y_all, 1)
            dve.wait_ge(fw_in, 16)
            for t in range(NT):
                dve.wait_ge(rms3, t + 1)
                link(w.reciprocal(ssum[:, 4 + t:5 + t], ssum[:, 2 + t:3 + t]))
                w.scalar_tensor_tensor(out=h[:, t, :], in0=pair(2 + t), scalar=ssum[:, 4 + t:5 + t], in1=wrow[:],
                                       op0=ALU.mult, op1=ALU.mult).then_inc(y_ok, 1)

        @block.tensor
        def _(pe):
            mm, tr = nc.tensor.matmul, nc.tensor.transpose
            pe.wait_ge(c_in, 16)
            pe.wait_ge(p_in, 32)
            tr(ps[:, 0, 0:TAPS * CH], rows[0:TAPS * CH, 0, :], ident[0:TAPS * CH, 0:TAPS * CH])
            tr(ps[:, 0, P:P + PRM], rows[0:PRM, 1, :], ident[0:PRM, 0:PRM]).then_inc(prm_ps, 1)
            pe.wait_ge(xn_ok, NT)
            for c in range(C):
                for t in range(NT):
                    last = tr(ps[:, 4 + c // 2, (c % 2) * T + t * P:(c % 2) * T + (t + 1) * P],
                              n2[:, t, c * P:(c + 1) * P], ident)
                if c % 2:
                    last.then_inc(xT_ok, 1)
            pe.wait_ge(nT_act, C // 2)
            pe.wait_ge(nT_dve, C // 2)

            def project_part(i, part):
                wt = ring[:, i % SLOTS]
                base = 2 * (i % 2)
                for c in range(C):
                    if i == IV:
                        last = mm(ps[:, base + part, :], nT[:, c, part * P:(part + 1) * P], wt[:, c, :],
                                  start=(c == 0), stop=(c == C - 1))
                    else:
                        o = (part % 2) * T
                        last = mm(ps[:, base + part // 2, o:o + T], wt[:, c, part * P:(part + 1) * P],
                                  nT[:, c, :], start=(c == 0), stop=(c == C - 1))
                return last

            def begin(i):
                for half in (0, 1):
                    pe.wait_ge(full[i % SLOTS][half], 16 * (i // SLOTS + 1))
                if i >= 2:
                    pe.wait_ge(ev_act, i - 1)
                    if i - 2 == QZ:
                        pe.wait_ge(ev_dve, 2)

            def products(k):
                pe.wait_ge(w_ok, max(2 * k + 1, 1))
                if k == 0:
                    pe.wait_ge(ev_dve, 2)
                if k >= 2:
                    pe.wait_ge(lev, k - 1)
                keys = wk[:, k % 2, 0]
                queries = wk[:, k % 2, 1] if k else q[:]
                for hd in range(H):
                    for t in range(NT):
                        if k == 1:
                            a, tq = t * H + hd, 1 - t
                        else:
                            a, tq = hd * NT + t, t
                        last = mm(ps[:, 4 + 2 * (k % 2) + a // 4, (a % 4) * P:(a % 4 + 1) * P],
                                  keys[:, hd, t * P:(t + 1) * P], queries[:, hd, tq * P:(tq + 1) * P],
                                  start=True, stop=True)
                last.then_inc(prod, 1)

            def mean():
                pe.wait_ge(conv_ok, TAPS * (CH - 1))
                pe.wait_ge(tap_sum, TAPS - 1)
                pe.wait_ge(ev_act, IV + 1)
                for c in range(CH):
                    last = mm(ps[:, 3, 0:T], ones_c[:], acc[:, c, :], start=(c == 0), stop=(c == CH - 1))
                last.then_inc(mu_ps, 1)

            def variance():
                pe.wait_ge(xc2_ok, 1)
                for c in range(CH):
                    last = mm(ps[:, 3, T:2 * T], ones_c[:], u[:, c, 0:T], start=(c == 0), stop=(c == CH - 1))
                last.then_inc(var_ps, 1)

            def project(i, then={}):
                begin(i)
                parts = NT if i == IV else 4
                for part in range(parts):
                    last = project_part(i, part)
                    if part == parts - 1:
                        last.then_inc(proj, 1)
                    for other in then.get(part, ()):
                        if isinstance(other, int):
                            products(other)
                        else:
                            other()

            def b1_to_columns():
                pe.wait_ge(b1_in, 16)
                for c in range(2 * C):
                    last = tr(ps[:, 4, c * E:(c + 1) * E], b1_rows[:, c * P:(c + 1) * P], ident[0:E, 0:E])
                last.then_inc(prm_ps, 1)

            def out_part(t, half, lo, hi):
                for c in range(lo, hi):
                    last = mm(ps[:, (4, 2)[half] + t, :], cat[:, c, t * P:(t + 1) * P],
                              ring[:, (N_IN + half) % SLOTS, c, :], start=(c == 4), stop=(c == 3))
                return last

            project(CV)
            project(CG)
            project(FF)
            b1_to_columns()
            project(FB)
            project(QZ)
            pe.wait_ge(prm_sb, 3)
            project(IV, {0: [0, 1], 1: [2, 3]})
            project(GZ, {0: [mean, 4], 1: [variance, 5], 2: [6], 3: [7]})
            products(8)
            pe.wait_ge(catb_ok, 1)
            for half in (0, 1):
                pe.wait_ge(full[(N_IN + 1) % SLOTS][half], 32)
            out_part(0, 1, 4, 8)
            pe.wait_ge(lev, N_STEP)
            pe.wait_ge(ev_dve, 3)
            for hd in range(H):
                vs = [v[:, t, hd * P:(hd + 1) * P] for t in range(NT)]
                for t in range(NT):
                    o = (hd % 2) * T + t * P
                    mm(ps[:, hd // 2, o:o + P], vs[t], am[:, hd, t, :], start=True, stop=False)
                    last = mm(ps[:, hd // 2, o:o + P], vs[1 - t], off[:, 1 - t, hd, :], start=False, stop=True)
            last.then_inc(av, 1)
            out_part(1, 1, 4, 8)
            pe.wait_ge(o2_ok, 1)
            for a in range(H * NT):
                last = mm(ps[:, 6, a:a + 1], wk[:, 1, 0, a // NT, (a % NT) * P:(a % NT + 1) * P], ones_v[:, 0:1],
                          start=True, stop=True)
            last.then_inc(oms_ps, 1)
            for half in (0, 1):
                pe.wait_ge(full[N_IN % SLOTS][half], 32)
            out_part(0, 0, 4, 8)
            pe.wait_ge(orec_ok, 1)
            for a in range(H * NT):
                last = mm(ps[:, 6 + a // 4, (a % 4) * P:(a % 4 + 1) * P], orms[:, 8 + a:9 + a].to_broadcast([P, P]),
                          ident, start=True, stop=True)
            last.then_inc(obc_ps, 1)
            out_part(1, 0, 4, 8)

            def n2_to_columns(t):
                pe.wait_ge(n2_ok, t + 1)
                for c in range(C):
                    last = tr(ps[:, 6 * t + c // 4, (c % 4) * P:(c % 4 + 1) * P], n2[:, t, c * P:(c + 1) * P], ident)
                last.then_inc(n2T_ps, 1)

            def logits(t):
                pe.wait_ge(n2T_sb, t + 1)
                pe.wait_ge(n2T_dve, t + 1)
                o = ps[:, 2, t * E:(t + 1) * E]
                for c in range(C):
                    mm(o, nT[:, c, t * P:(t + 1) * P], rw[:, c, :], start=(c == 0), stop=False)
                last = mm(o, ones[0:1, 0:P], rb[:], start=False, stop=True)
                last.then_inc(lgt_ps, 1)

            def keep_clock():
                mm(ps[:, 5, :], ident, cst[:, 0:512], start=True, stop=True)

            def start_sums(t, half):
                mm(ps[:, 4 + 2 * t + half, :], ident, h[:, t, half * CW:(half + 1) * CW], start=True, stop=False)

            pe.wait_ge(cata_ok, 1)
            out_part(0, 0, 0, 4).then_inc(oproj, 1)
            out_part(0, 1, 0, 4).then_inc(oproj, 1)
            out_part(1, 0, 0, 4).then_inc(oproj, 1)
            n2_to_columns(0)
            out_part(1, 1, 0, 4).then_inc(oproj, 1)
            pe.wait_ge(r_in, 32)
            logits(0)
            pe.wait_ge(h_ok, NT)
            keep_clock()
            n2_to_columns(1)
            logits(1)
            start_sums(0, 0)
            start_sums(0, 1)
            pe.wait_ge(sel_ok, 1)
            s = rt[:, 7]
            mm(ps[:, 2, 64:64 + E], tri, s[:, 0, :], start=True, stop=True)
            mm(ps[:, 2, 96:96 + E], tri, s[:, 1, :], start=True, stop=False)
            mm(ps[:, 2, 96:96 + E], ones[:, 0:P], s[:, 0, :], start=False, stop=True)
            mm(ps[:, 2, P:P + E], ones[:, 0:P], s[:, 0, :], start=True, stop=False)
            mm(ps[:, 2, P:P + E], ones[:, 0:P], s[:, 1, :], start=False, stop=True).then_inc(rank_ps, 1)
            pe.wait_ge(gates_ok, 1)
            for t in range(NT):
                last = tr(ps[0:E, 0, t * P:(t + 1) * P], gates[:, t, :], ident)
            last.then_inc(gT_ps, 1)
            start_sums(1, 0)
            def gather(n, part):
                pe.wait_ge(s_sel, n + 1)
                for c in range(4 * part, 4 * part + 4):
                    for t in range(NT):
                        last = mm(ps[:, 3, c * BLK:(c + 1) * BLK], n2[:, t, c * P:(c + 1) * P], sel[:, t, :],
                                  start=(t == 0), stop=(t == NT - 1))
                if part == 1:
                    last.then_inc(s_xps, 1)

            def multiply(n, uu):
                j, half = ORDER[uu]
                if half == 0:
                    if not (isinstance(n, int) and n == 0 and j < 2):
                        pe.wait_ge(s_ev, N_EXP * n + j - 1)
                    if j == 0:
                        pe.wait_ge(s_xl, n + 1)
                if j >= 4:
                    pe.wait_ge(s_al, 2 * n + half + 1)
                lhs = xg if j < 4 else aT
                for part, src, ready in ((0, wh, s_wh), (1, wl, s_wl)):
                    pe.wait_ge(ready, UNITS * n + uu + 1)
                    for c in range(4):
                        if part == 1 and c == DG:
                            pe.wait_ge(s_wp, UNITS * n + uu + 1)
                        last = mm(ps[:, j % 2, :], lhs[:, 4 * half + c, :], src[:, uu % WD, c, :],
                                  start=(half == 0 and part == 0 and c == 0),
                                  stop=(half == 1 and part == 1 and c == 3))
                last.then_inc(s_mm, 1)

            def transpose_sum(n, j):
                pe.wait_ge(s_ev, N_EXP * n + j + 1)
                if j == 0 and not (isinstance(n, int) and n == 0):
                    pe.wait_ge(s_pre, 2 * n)
                if j == 2:
                    pe.wait_ge(s_pre, 2 * n + 1)
                for c in range(4):
                    o = (j % 2) * 4 * BLK + c * BLK
                    last = mm(ps[:, 2, o:o + BLK], hid[:, j % 2, c * P:(c + 1) * P], ident2, start=True, stop=True)
                last.then_inc(s_tr, 1)

            def gates_to_rows(n):
                pe.wait_ge(s_selg, n + 1)
                pe.wait_ge(s_xl, n + 1)
                for t in range(NT):
                    last = tr(ps[:, 3, t * P:(t + 1) * P], selg[:, t].rearrange("p a b -> p (a b)"), ident)
                last.then_inc(s_gps, 1)

            def combine(n, piece):
                half, t = piece // 2, piece % 2
                if piece == 0:
                    pe.wait_ge(s_gt, n + 1)
                if t == 0:
                    pe.wait_ge(s_ev, N_EXP * n + 5 + half)
                mm(ps[:, 4 + 2 * t + half, :], gsel[:, t, :], y[:, half * CW:(half + 1) * CW],
                   start=False, stop=True, skip_group_check=True).then_inc(s_comb, 1)

            def body(n, before, following, first=False):
                for uu in range(UNITS):
                    multiply(n, uu)
                    if uu == 1 and before:
                        gates_to_rows(n - 1)
                    if uu == 2:
                        transpose_sum(n, 0)
                    if uu == 3 and first:
                        add_biases(1)
                    if uu == 4:
                        transpose_sum(n, 1)
                    if uu == 5 and before:
                        combine(n - 1, 0)
                    if uu == 6:
                        transpose_sum(n, 2)
                    if uu == 7:
                        if before:
                            combine(n - 1, 1)
                        transpose_sum(n, 3)
                        if following:
                            gather(n + 1, 0)
                        if first:
                            gather(n + 1, 1)
                    if uu == 8:
                        if following and not first:
                            gather(n + 1, 1)
                        if before:
                            combine(n - 1, 2)
                            combine(n - 1, 3)
                        if first:
                            add_biases(2)
                    if uu == 9 and first:
                        start_sums(1, 1)
                        add_biases(3)
                    if uu == 10 and not following:
                        gates_to_rows(n)

            def add_biases(piece):
                if piece == 0:
                    pe.wait_ge(gT_sb, 1)
                    pe.wait_ge(b2_in, 16)
                half, t = piece // 2, piece % 2
                mm(ps[:, 4 + 2 * t + half, :], gT[:, t * P:(t + 1) * P], b2_rows[:, half * CW:(half + 1) * CW],
                   start=False, stop=True)

            def finish(n):
                for piece in range(NPC):
                    combine(n, piece)

            gather(0, 0)
            gather(0, 0)
            gather(0, 1)
            add_biases(0)
            body(0, False, True, True)
            with pe.Fori(1, E - 1) as n:
                body(n, True, True)
            body(E - 1, True, False)
            finish(E - 1)
            pe.wait_ge(tabled, 1)
            n_more = pe.value_load(nextra[0:1, 0:1], min_val=0, max_val=EXTRA)
            with pe.If(n_more > 0):
                with pe.Fori(0, EXTRA) as i:
                    with pe.If(i < n_more):
                        gather(E + i, 0)
                        gather(E + i, 1)
                        body(E + i, False, False)
                        finish(E + i)
                    pe.nop()
            tr(ps[:, 2, 0:P], ident, ident).then_inc(y_all, 1)


def constants():
    import numpy as np
    c = np.zeros((P, K_END), np.float32)
    c[:, K_ID:K_ID + P] = np.eye(P)
    c[:, K_ID2:K_ID2 + BLK] = np.tile(np.eye(BLK), (2, 1))
    c[:, K_IOTA:K_IOTA + T] = np.arange(T)
    s, t = np.arange(P)[:, None], np.arange(P)[None, :]
    c[:, K_TRI:K_TRI + P] = s < t
    m = np.zeros((P, N_MASK, P), np.float32)
    m[:, 0, :] = s == t
    for i, h in enumerate(LEVELS[1:]):
        m[:, i + 1, :] = (s // (2 * h) == t // (2 * h)) & (s // h != t // h)
    return c, m


def kernel(x, norm1_w, w_in, lb_logits, hgrn_norm_w, dw_w, dw_b, conv_ln_w, conv_ln_b,
           w_out, norm2_w, router_w, router_b, w1, b1, w2, b2, final_norm_w):
    import numpy as np
    import concourse.bacc as bacc
    from concourse.bass_utils import run_bass_kernel_spmd
    c, m = constants()
    rows = lambda a: np.asarray(a).reshape(-1, P)
    ins = {
        "x": np.asarray(x)[0], "w_in": np.asarray(w_in)[0],
        "w_out": np.asarray(w_out)[0], "w1": np.asarray(w1)[0], "w2": np.asarray(w2)[0],
        "prm": np.concatenate([rows(lb_logits), rows(dw_b), rows(conv_ln_w), rows(conv_ln_b), rows(hgrn_norm_w),
                               rows(norm1_w)]),
        "dww": rows(dw_w), "b1": np.asarray(b1)[0], "b2": np.asarray(b2)[0],
        "router_w": np.asarray(router_w)[0], "router_b": np.asarray(router_b)[0],
        "norm2_w": np.asarray(norm2_w)[0], "final_w": np.asarray(final_norm_w), "consts": c, "masks": m,
    }
    ins = {k: np.ascontiguousarray(a) for k, a in ins.items()}
    nc = bacc.Bacc("TRN2", target_bir_lowering=False, num_devices=1)
    args = {k: nc.dram_tensor("in_" + k, a.shape, mybir.dt.from_np(a.dtype), kind="ExternalInput").ap()
            for k, a in ins.items()}
    out = nc.dram_tensor("out", (T, D), F32, kind="ExternalOutput").ap()
    encoder_layer(nc, out=out, **args)
    r = run_bass_kernel_spmd(nc, [{"in_" + k: a for k, a in ins.items()}], core_ids=[0])
    return r.results[0]["out"].reshape(1, T, D)
```
